# Optimizing a Trainium2 kernel written in Bass

```python
import jax, jax.numpy as jnp
from jax import lax
import numpy as np

D_MODEL = 1024
BATCH = 1
SEQ = 2048
DEPTH = 1

CHUNK = 64
D_MIX = D_MODEL
EPS = 1e-5
NEG = -1e30
F_FLOOR = 1e-6

A_DK = 128
A_DV = 128
A_WIDTH = D_MIX // 2
A_HEADS = A_WIDTH // A_DV
A_CHUNK = 16

POOL_WINDOWS = (2, 4, 8, 16)
B_GROUPS = 4
B_WIDTH = D_MIX // 4
B_GDIM = B_WIDTH // B_GROUPS

C_WIDTH = D_MIX - A_WIDTH - B_WIDTH
C_HEAD_DIM = 64
C_Q_HEADS = C_WIDTH // C_HEAD_DIM
C_KV_HEADS = 2
C_KV_WIDTH = C_KV_HEADS * C_HEAD_DIM
WINDOW = 128
N_PREV_CHUNKS = WINDOW // CHUNK - 1

D_IN = 3 * A_WIDTH + B_WIDTH + C_WIDTH + 2 * C_KV_WIDTH + D_MIX

ALPHA = (2.0 * DEPTH) ** 0.25
BETA = (8.0 * DEPTH) ** -0.25

kernel_name = 'hybrid_hgrn2_pool_swa_sink_deepnorm'

def _split_columns(h):
    widths = (A_WIDTH, A_WIDTH, A_WIDTH, B_WIDTH, C_WIDTH, C_KV_WIDTH, C_KV_WIDTH, D_MIX)
    parts = []
    start = 0
    for w in widths:
        parts.append(h[..., start:start + w])
        start += w
    return parts

def hgrn2_mixer(q, f_logit, i, lb, gain):
    bsz, seq, _ = q.shape
    n = seq // A_CHUNK
    f32 = jnp.float32
    shp = (bsz, n, A_CHUNK, A_HEADS, A_DK)
    lb = lb.astype(f32).reshape(A_HEADS, A_DK)
    qf = jax.nn.silu(q.astype(f32)).reshape(shp)
    z = f_logit.astype(f32).reshape(shp)
    f = lb + (1.0 - lb) * jax.nn.sigmoid(z)
    k = (1.0 - lb) * jax.nn.sigmoid(-z)
    log_f = jnp.log(jnp.maximum(f, F_FLOOR))
    v = i.astype(f32).reshape(bsz, n, A_CHUNK, A_HEADS, A_DV)
    b = jnp.cumsum(log_f, axis=2)
    b_last = b[:, :, A_CHUNK - 1:A_CHUNK]
    causal = jnp.tril(jnp.ones((A_CHUNK, A_CHUNK), dtype=bool))[None, None, :, :, None, None]
    diff = b[:, :, :, None] - b[:, :, None, :]
    decay_ts = jnp.exp(jnp.where(causal, diff, NEG))
    scores = jnp.einsum('bnthd,bnshd,bntshd->bnhts', qf, k, decay_ts)
    o_intra = jnp.einsum('bnhts,bnshv->bnthv', scores, v)
    u = jnp.einsum('bnshd,bnshv->bnhdv', k * jnp.exp(b_last - b), v)
    decay = jnp.exp(b_last[:, :, 0])

    def step(state, inp):
        d, uc = inp
        return d[..., None] * state + uc, state

    s0 = jnp.zeros((bsz, A_HEADS, A_DK, A_DV), f32)
    _, s_start = lax.scan(step, s0, (jnp.moveaxis(decay, 1, 0), jnp.moveaxis(u, 1, 0)))
    s_start = jnp.moveaxis(s_start, 0, 1)
    o_inter = jnp.einsum('bnthd,bnhdv->bnthv', qf * jnp.exp(b), s_start)
    o = (o_intra + o_inter).reshape(bsz, seq, A_HEADS, A_DV)
    o = o * lax.rsqrt(jnp.mean(jnp.square(o), axis=-1, keepdims=True) + EPS)
    o = o * gain.astype(f32).reshape(A_HEADS, A_DV)
    return o.reshape(bsz, seq, A_WIDTH)

def pool_mixer(u, pool_w, pool_scale):
    bsz, seq, _ = u.shape
    f32 = jnp.float32
    u32 = u.astype(f32)
    csum = jnp.cumsum(u32, axis=1)
    count_base = jnp.arange(1, seq + 1, dtype=f32)
    groups = []
    for g, w in enumerate(POOL_WINDOWS):
        cg = csum[..., g * B_GDIM:(g + 1) * B_GDIM]
        prev = jnp.pad(cg, ((0, 0), (w, 0), (0, 0)))[:, :seq]
        count = jnp.minimum(count_base, float(w))[None, :, None]
        groups.append((cg - prev) / count - u32[..., g * B_GDIM:(g + 1) * B_GDIM])
    pooled = jnp.stack(groups, axis=2)
    mixed = jnp.einsum('bsgi,gio->bsgo', pooled, pool_w.astype(f32))
    return mixed.reshape(bsz, seq, B_WIDTH) * pool_scale.astype(f32)

def swa_sink_mixer(q, k, v, sinks):
    bsz, seq, _ = q.shape
    n = seq // CHUNK
    grp = C_Q_HEADS // C_KV_HEADS
    f32 = jnp.float32
    qh = q.astype(f32).reshape(bsz, n, CHUNK, C_KV_HEADS, grp, C_HEAD_DIM)
    kh = k.astype(f32).reshape(bsz, n, CHUNK, C_KV_HEADS, C_HEAD_DIM)
    vh = v.astype(f32).reshape(bsz, n, CHUNK, C_KV_HEADS, C_HEAD_DIM)

    def band(t):
        pads = [(0, 0)] * t.ndim
        parts = []
        for j in range(N_PREV_CHUNKS, 0, -1):
            pads_j = list(pads)
            pads_j[1] = (j, 0)
            parts.append(jnp.pad(t, pads_j)[:, :n])
        return jnp.concatenate(parts + [t], axis=2)

    kb, vb = band(kh), band(vh)
    offsets = jnp.repeat(jnp.arange(N_PREV_CHUNKS, -1, -1), CHUNK)
    valid = (jnp.arange(n)[:, None] - offsets[None, :]) >= 0
    s = jnp.einsum('bnqkgd,bnskd->bnkgqs', qh, kb) * (C_HEAD_DIM ** -0.5)
    s = jnp.where(valid[None, :, None, None, None, :], s, NEG)
    sink = sinks.astype(f32).reshape(C_KV_HEADS, grp)[None, None, :, :, None, None]
    m = jnp.maximum(jnp.max(s, axis=-1, keepdims=True), sink)
    p = jnp.exp(s - m)
    denom = jnp.sum(p, axis=-1, keepdims=True) + jnp.exp(sink - m)
    o = jnp.einsum('bnkgqs,bnskd->bnqkgd', p / denom, vb)
    return o.reshape(bsz, seq, C_WIDTH)

def layer_norm(x, gain, bias):
    x32 = x.astype(jnp.float32)
    mu = jnp.mean(x32, axis=-1, keepdims=True)
    var = jnp.mean(jnp.square(x32 - mu), axis=-1, keepdims=True)
    return (x32 - mu) * lax.rsqrt(var + EPS) * gain.astype(jnp.float32) + bias.astype(jnp.float32)

def setup_inputs(seed: int = 0) -> dict:
    key = jax.random.key(seed)
    ks = jax.random.split(key, 12)
    f32 = jnp.float32
    x = jax.random.normal(ks[0], (BATCH, SEQ, D_MODEL), f32)
    w_in = jax.random.normal(ks[1], (DEPTH, D_MODEL, D_IN), f32) * D_MODEL ** -0.5
    b_in = 0.02 * jax.random.normal(ks[2], (DEPTH, D_IN), f32)
    lb_logits = 0.5 * jax.random.normal(ks[3], (DEPTH, A_WIDTH), f32)
    a_norm_gain = 1.0 + 0.05 * jax.random.normal(ks[4], (DEPTH, A_WIDTH), f32)
    pool_w = jax.random.normal(ks[5], (DEPTH, B_GROUPS, B_GDIM, B_GDIM), f32) * B_GDIM ** -0.5
    pool_scale = 1.0 + 0.05 * jax.random.normal(ks[6], (DEPTH, B_WIDTH), f32)
    attn_sinks = 0.5 * jax.random.normal(ks[7], (DEPTH, C_Q_HEADS), f32)
    w_out = jax.random.normal(ks[8], (DEPTH, D_MIX, D_MODEL), f32) * (D_MIX ** -0.5) * BETA
    b_out = 0.02 * jax.random.normal(ks[9], (DEPTH, D_MODEL), f32)
    ln_gain = 1.0 + 0.05 * jax.random.normal(ks[10], (DEPTH, D_MODEL), f32)
    ln_bias = 0.02 * jax.random.normal(ks[11], (DEPTH, D_MODEL), f32)
    return {'x': x, 'w_in': w_in, 'b_in': b_in, 'lb_logits': lb_logits,
            'a_norm_gain': a_norm_gain, 'pool_w': pool_w, 'pool_scale': pool_scale,
            'attn_sinks': attn_sinks, 'w_out': w_out, 'b_out': b_out,
            'ln_gain': ln_gain, 'ln_bias': ln_bias}

def reference(x, w_in, b_in, lb_logits, a_norm_gain, pool_w, pool_scale, attn_sinks,
              w_out, b_out, ln_gain, ln_bias):
    dtype = x.dtype
    p = jax.nn.softmax(lb_logits.astype(jnp.float32), axis=0)
    lower_bounds = jnp.maximum(jnp.cumsum(p, axis=0) - p[0:1], 0.0)
    for l in range(DEPTH):
        h = jnp.einsum('bsd,de->bse', x, w_in[l]) + b_in[l]
        qa, fa, ia, ub, qc, kc, vc, z = _split_columns(h)
        o_a = hgrn2_mixer(qa, fa, ia, lower_bounds[l], a_norm_gain[l])
        o_b = pool_mixer(ub, pool_w[l], pool_scale[l])
        o_c = swa_sink_mixer(qc, kc, vc, attn_sinks[l])
        mix = jnp.concatenate([o_a, o_b, o_c], axis=-1) * jax.nn.silu(z.astype(jnp.float32))
        y = jnp.einsum('bse,ed->bsd', mix.astype(dtype), w_out[l]) + b_out[l]
        x = layer_norm(ALPHA * x + y, ln_gain[l], ln_bias[l]).astype(dtype)
    return x


_drawn_inputs = setup_inputs


def setup_inputs(seed=0):
    import zlib

    import numpy as np

    out = dict(_drawn_inputs(seed))
    spreads = {}
    factors = {'b_in': 6.34,
     'a_norm_gain': 5.684,
     'pool_scale': 8.0,
     'attn_sinks': 8.0,
     'b_out': 3.5,
     'ln_bias': 2.835}
    for name, (base, spread) in spreads.items():
        noise = np.random.default_rng([zlib.crc32(name.encode()), seed]).standard_normal(out[name].shape)
        drawn = base * np.exp(spread * noise) if base else spread * noise
        out[name] = __import__('jax').numpy.asarray(drawn.astype(out[name].dtype))
    for name, factor in factors.items():
        out[name] = (out[name] * factor).astype(out[name].dtype)
    return out
```

```python
from contextlib import ExitStack

import numpy as np

import concourse.bass as bass
from concourse import mybir

F32 = mybir.dt.float32
F32R = mybir.dt.float32r
I32 = mybir.dt.int32
ALU = mybir.AluOpType
ACT = mybir.ActivationFunctionType
AX = mybir.AxisListType

P = 128
D = 1024
SEQ = 2048
TB = 512
BLOCKS = SEQ // TB
KT = D // P
A_HEADS, B_TILES, KV = 4, 2, 2
HD = 64
EPS = 1e-5
F_FLOOR = 1e-6
NEG = -1e30
ALPHA = 2.0 ** 0.25
SCALE = HD ** -0.5
EXP_CAP = 2.0 ** 60
POOL_WINDOWS = (2, 4, 8, 16)
PAD = 16
CHUNK = 128
CHUNKS = TB // CHUNK
PAIRS = TB // P
LEVELS = (8, 16, 32, 64)

IN_UNITS = 26
OUT_UNITS = 8
UNITS = IN_UNITS + OUT_UNITS
XP = KT // 2
ROWS = TB // P

U_CQ, U_CK, U_CV, U_B = 0, 2, 3, 4
U_HEAD = (6, 10, 14, 18)
U_GATE = (9, 13, 17, 21, 22, 23, 24, 25)
CHAINS = tuple(sorted(U_GATE + U_HEAD + tuple(u + 1 for u in U_HEAD)))
M_C, M_B, M_A = 0, 2, 4

PR_BIN, PR_LB, PR_GAIN, PR_PSC, PR_SINK = 0, 26, 30, 34, 36
PR_N = 40
K_ID, K_MEAN, K_R16, K_R128, K_PEN, K_CORR, K_WINV, K_MASK = 0, 128, 256, 768, 1280, 1408, 1440, 1442
K_N = K_MASK + 128 + 4 * 64


def column_order():
    a, b, c, kv = 512, 256, 256, 128
    q0, f0, i0 = 0, a, 2 * a
    u0 = 3 * a
    c0 = u0 + b
    k0, v0, z0 = c0 + c, c0 + c + kv, c0 + c + 2 * kv

    def heads(base, g):
        return np.concatenate([base + (j * 2 + g) * HD + np.arange(HD) for j in range(KV)])

    tiles = [heads(c0, 0), heads(c0, 1), k0 + np.arange(P), v0 + np.arange(P)]
    tiles += [u0 + t * P + np.arange(P) for t in range(B_TILES)]
    tiles += [None] * (IN_UNITS - len(tiles))
    for h, u in enumerate(U_HEAD):
        tiles[u:u + 3] = [base + h * P + np.arange(P) for base in (f0, q0, i0)]
    for u, m in zip(U_GATE, mixing_order()):
        tiles[u] = z0 + m
    return tiles


def mixing_order():
    tiles = [2 * 256 + 256 + np.concatenate([(j * 2 + g) * HD + np.arange(HD) for j in range(KV)]) for g in range(2)]
    tiles += [512 + t * P + np.arange(P) for t in range(B_TILES)]
    return tiles + [h * P + np.arange(P) for h in range(A_HEADS)]


def constants():
    k = np.zeros((P, K_N), np.float32)
    t = np.arange(TB)
    k[:, K_ID:K_ID + P] = np.eye(P)
    k[:, K_MEAN:K_MEAN + P] = 1.0 / P
    k[:, K_R16:K_R16 + TB] = t % 16 != 0
    k[:, K_R128:K_R128 + TB] = t % CHUNK != 0
    k[0:HD, K_PEN:K_PEN + HD] = NEG
    for g, w in enumerate(POOL_WINDOWS):
        rows = slice((g % 2) * HD, (g % 2) * HD + HD)
        k[rows, K_CORR + (g // 2) * PAD:K_CORR + (g // 2 + 1) * PAD] = w / np.minimum(np.arange(PAD) + 1, w)
        k[rows, K_WINV + g // 2] = 1.0 / w
    s, tt = np.arange(P)[:, None], np.arange(P)[None, :]
    k[:, K_MASK:K_MASK + P] = (s // 8 == tt // 8) & (s <= tt)
    for n, lv in enumerate(LEVELS):
        upper = (tt // lv % 2 == 1)[0]
        m = (s // (2 * lv) == tt // (2 * lv)) & (s // lv % 2 == 0)
        k[:, K_MASK + P + 64 * n:K_MASK + P + 64 * (n + 1)] = m[:, upper]
    return k


def schedule():
    table = [([], []) for _ in range(UNITS)]
    MID, AFTER = 0, 1

    def put(n, half, *step):
        table[n][half].append(step)

    for h, u in enumerate(U_HEAD):
        for c in range(CHUNKS):
            put(u + 5 + c, MID, "chunk_out", h, c)
            put(u + 4 + c, MID, "chunk_scores", h, c)
        put(u + 8, AFTER, "norm", h)
    put(4, AFTER, "v_turn", 0)
    put(5, MID, "v_turn", 1)
    for p in range(PAIRS):
        put(7 + p, AFTER, "attend", p)
    for p in range(PAIRS):
        put(6 + p, MID, "normalise", p)
        put(6 + p, AFTER, "p_turn", p)
    for p in range(PAIRS):
        put(5 + p, AFTER, "logits", p)
    for t in range(B_TILES):
        put(6 + t, AFTER, "windows", t)
        put(8 + t, MID, "pool_mix", t)
    for c, u in enumerate(CHAINS):
        put(u + 1, MID, "sigmoid", c)
        put(u + (2 if u == U_GATE[-1] else 1), MID, "use_sigmoid", c)
    for h, u in enumerate(U_HEAD):
        put(u + 1, AFTER, "log_decay", h)
        put(u + 2, MID, "differences", h)
        put(u + 2, AFTER, "exponentials", h)
        put(u + 3, MID, "products", h)
    for s in range(ROWS):
        put(25 + s, AFTER, "residual", s)
    put(IN_UNITS + 3, AFTER, "take_rows", 0)
    put(IN_UNITS + 7, AFTER, "take_rows", 1)
    return table


def w_slot(u):
    u %= UNITS
    return 1 if u == UNITS - 1 else u % 3


HEAD_PIECES = [("w", 0)] + [("x", j) for j in range(XP)] + [("w", 1), ("w", 2)]
SPLITS = [[("w", n + 3)] for n in range(IN_UNITS)]
SPLITS += [[("x", XP + j), ("w", IN_UNITS + 3 + j)] for j in range(XP)]
SPLITS += [[], [("w", 33)], [("w", 34)], [("w", 35), ("w", 36)]]
BODY_PIECES = [p for after in SPLITS for p in after]
AHEAD_LOADS = 2


PER = {
    "unit_done": UNITS, "w_hi": UNITS, "w_lo": UNITS, "x_hi": XP, "x_lo": XP,
    "proj_taken": IN_UNITS, "e_ready": 16, "d_ready": 16, "sig_ready": 16, "sig_used": 8,
    "floored": A_HEADS, "logf_ready": A_HEADS, "diff_ready": 6 * A_HEADS, "exp_ready": 6 * A_HEADS,
    "prep_done": A_HEADS, "turned": 16, "scores_done": 16, "turn_taken": 16, "scores_taken": 16,
    "chunk_done": 16, "o_taken": 16, "state_ready": 16, "mean_done": A_HEADS, "mean_taken": A_HEADS,
    "inv_ready": A_HEADS, "norm_done": A_HEADS,
    "v_turned": 2, "v_taken": 2, "logits_done": PAIRS, "max_ready": PAIRS, "p_exp": PAIRS, "p_ready": PAIRS,
    "p_turned": PAIRS, "pt_taken": PAIRS, "attend_done": PAIRS, "attend_taken": PAIRS, "carry_done": 1,
    "pooled": B_TILES, "pool_done": B_TILES, "pool_taken": B_TILES,
    "mix_ready": KT, "x_in": 16 * ROWS, "y_taken": 2 * ROWS,
    "var_ready": 1, "rstd_ready": 1, "nmr_ready": 1, "normed": ROWS, "scaled": ROWS, "out_ready": ROWS, "out_landed": 16 * ROWS,
}
AHEAD = ("y_taken", "out_landed")


def trunk_kernel(nc, xt, xr, w, params, consts, pool_w, b_out, ln_gain, ln_bias, out):
    S_TABLE = schedule()
    with ExitStack() as ctx:
        def sb(name, shape, dt=F32):
            return ctx.enter_context(nc.sbuf_tensor(name, shape, dt))

        def bank(n):
            return ctx.enter_context(nc.psum_tensor(f"bank{n}", [P, 512], F32))

        sem = {name: ctx.enter_context(nc.semaphore(name)) for name in PER}
        raw_in = [ctx.enter_context(nc.semaphore(f"raw_in{i}")) for i in range(2)]
        params_in = ctx.enter_context(nc.semaphore("params_in"))
        dve_ready = ctx.enter_context(nc.semaphore("dve_setup"))
        act_ready = ctx.enter_context(nc.semaphore("act_setup"))
        dve_step = ctx.enter_context(nc.semaphore("dve_step"))
        act_step = ctx.enter_context(nc.semaphore("act_step"))

        banks = [bank(n) for n in range(8)]

        raw = [sb(f"raw{i}", [P, 1024]) for i in range(2)]
        w_hi = [sb(f"w_hi{i}", [P, 1024], F32R) for i in range(3)]
        w_lo = [sb(f"w_lo{i}", [P, 1024], F32R) for i in range(3)]
        xt_hi = sb("xt_hi", [P, KT, TB], F32R)
        xt_lo = sb("xt_lo", [P, KT, TB], F32R)
        mix_hi = sb("mix_hi", [P, KT, TB], F32R)
        mix_lo = sb("mix_lo", [P, KT, TB], F32R)
        mixed = sb("mixed", [P, KT, TB])
        par = sb("par", [P, PR_N])
        nbin = sb("nbin", [P, IN_UNITS])
        kc = sb("kc", [P, K_N])
        pw = sb("pw", [P, B_TILES, P])
        bout = sb("bout", [P, D])
        gain = sb("gain", [P, D])
        beta = sb("beta", [P, D])
        lb = sb("lb", [P, A_HEADS])
        lb_tmp = sb("lb_tmp", [P, 3, A_HEADS])
        one_lb = sb("one_lb", [P, A_HEADS])
        nsink = sb("nsink", [P, 4])
        eps = sb("eps", [P, 1])
        ident = kc[:, K_ID:K_ID + P]
        mean_w = kc[:, K_MEAN:K_MEAN + P]
        masks = kc[:, K_MASK:K_N].bitcast(I32)
        lin = [sb(f"lin{i}", [P, TB]) for i in range(2)]
        sig = [sb(f"sig{i}", [P, TB]) for i in range(2)]
        q = sb("q", [P, TB])
        k = sb("k", [P, TB])
        logf = sb("logf", [P, TB])
        b16 = sb("b16", [P, TB])
        b128 = logf
        heads = [sb(f"heads{i}", [P, 10, TB]) for i in range(2)]
        N_Q8, N_K8, N_L, N_QIN, N_KEND, N_EIN, N_V = 0, 1, 2, 6, 7, 8, 9
        state = sb("state", [P, A_HEADS, P])
        kv_nat = [sb(f"kv_nat{i}", [P, 2 * P]) for i in range(2)]
        sct = [sb(f"sct{i}", [P, P]) for i in range(2)]
        osq = [sb(f"osq{i}", [P, TB]) for i in range(2)]
        kt_ = sb("kt_", [P, HD + TB])
        vt_ = sb("vt_", [P, HD + TB])
        qt = [heads[1][:, i, :] for i in range(2)]
        v_win = [heads[1][:, 2 + i, :] for i in range(2)]
        prob = [heads[1][:, 4 + i, :] for i in range(2)]
        pt = heads[1][:, 6, :]
        cmax = sb("cmax", [P, 2, 4])
        nm = sb("nm", [P, 2, 4])
        es = sb("es", [P, 2, 4])
        den = sb("den", [P, 2, 4])
        rden = sb("rden", [P, 2, 4])
        ub = sb("ub", [P, B_TILES, PAD + TB])
        spare = heads[1][:, 7:10, :].rearrange("p a t -> p (a t)")
        win = [spare[:, i * (PAD + TB):(i + 1) * (PAD + TB)] for i in range(2)]
        pooled = osq
        rows = heads[0][:, 0:8, :].rearrange("p (s h) t -> p s (h t)", s=ROWS)
        stats = sb("stats", [P, ROWS, 2, 6])
        mv = sb("mv", [P, ROWS, 2])
        rstd = sb("rstd", [P, ROWS])
        nmr = sb("nmr", [P, ROWS])

        def nth(b, name, n):
            return b * PER[name] + (n + (PER[name] if name in AHEAD else 0))

        def nth_before(b, name, n):
            return b * PER[name] + n

        def used_event(n):
            if n in U_GATE:
                return "mix_ready", U_GATE.index(n) + 1
            return "sig_used", 1 + [u for u in CHAINS if u not in U_GATE].index(n)

        block = ctx.enter_context(nc.Block())

        @block.sync
        def _(sp):
            pieces = HEAD_PIECES + BODY_PIECES + BODY_PIECES[:AHEAD_LOADS]

            def load(b, i):
                kind, n = pieces[i]
                if i >= 2:
                    k2, n2 = pieces[i - 2]
                    if b is None:
                        sp.wait_ge(sem[f"{k2}_lo"], n2 + 1)
                    else:
                        if i - 2 >= len(HEAD_PIECES) + len(BODY_PIECES):
                            n2 += PER[f"{k2}_lo"]
                        sp.wait_ge(sem[f"{k2}_lo"], nth(b, f"{k2}_lo", n2 + 1))
                if kind == "w":
                    src = w[n % UNITS]
                elif n < XP:
                    src = xt[0, n]
                else:
                    src = xt[b + 1, n - XP]
                sp.dma_start(raw[i % 2][:], src).then_inc(raw_in[i % 2], 16)

            for i in range(len(HEAD_PIECES) + AHEAD_LOADS):
                load(None, i)
            with sp.Fori(0, BLOCKS) as b:
                for i in range(len(HEAD_PIECES) + AHEAD_LOADS, len(pieces)):
                    load(b, i)
                    if pieces[i] == ("w", 26):
                        sp.wait_ge(sem["chunk_done"], nth(b, "chunk_done", 12))
                        sp.wait_ge(sem["out_landed"], nth_before(b, "out_landed", 16 * ROWS))
                    if pieces[i] in (("w", 26), ("w", 27)):
                        for s in range(2 * pieces[i][1] - 52, 2 * pieces[i][1] - 50):
                            sp.dma_start(rows[:, s, :], xr[b, s]).then_inc(sem["x_in"], 16)
                for s in range(ROWS):
                    sp.wait_ge(sem["out_ready"], nth(b, "out_ready", s + 1))
                    sp.dma_start(out[b, s], rows[:, s, :]).then_inc(sem["out_landed"], 16)
            sp.wait_ge(sem["out_landed"], PER["out_landed"] * (BLOCKS + 1))
            total = len(HEAD_PIECES) + AHEAD_LOADS + BLOCKS * len(BODY_PIECES)
            for i in range(2):
                sp.wait_ge(raw_in[i], 16 * ((total + 1 - i) // 2))

        @block.gpsimd
        def _(pool):
            pool.sem_inc(sem["out_landed"], PER["out_landed"])
            with pool.Fori(0, BLOCKS) as b:
                for s in range(ROWS):
                    pool.wait_ge(sem["scaled"], nth(b, "scaled", s + 1))
                    nc.gpsimd.tensor_tensor(rows[:, s, :], rows[:, s, :], beta[:], ALU.add).then_inc(sem["out_ready"], 1)

        @block.tensor
        def _(pe):
            def project(b, n, mid):
                o = banks[n % 2]
                ws = w_slot(n)
                pe.wait_ge(sem["w_lo"], nth(b, "w_lo", n + 1))
                if n < 2:
                    pe.wait_ge(sem["y_taken"], nth_before(b, "y_taken", n + 1))
                else:
                    pe.wait_ge(sem["proj_taken"], nth(b, "proj_taken", n - 1))
                for kt in range(KT):
                    if n == 0 and kt % 2 == 0:
                        pe.wait_ge(sem["x_lo"], nth(b, "x_lo", kt // 2 + 1))
                    if kt == KT // 2:
                        mid()
                    c = slice(kt * P, kt * P + P)
                    for step, (wx, xx) in enumerate(((w_hi, xt_hi), (w_hi, xt_lo), (w_lo, xt_hi))):
                        mm = nc.tensor.matmul(o[:], wx[ws][:, c], xx[:, kt, :],
                                              start=(kt == 0 and step == 0), stop=(kt == KT - 1 and step == 2))
                mm.then_inc(sem["unit_done"], 1)

            def project_out(b, n, mid):
                half, kp = divmod(n - IN_UNITS, 4)
                ws = w_slot(n)
                pe.wait_ge(sem["w_lo"], nth(b, "w_lo", n + 1))
                pe.wait_ge(sem["mix_ready"], nth(b, "mix_ready", 2 * kp + 2))
                if half == 0 and kp == 0:
                    pe.wait_ge(sem["proj_taken"], nth(b, "proj_taken", IN_UNITS))
                    pe.wait_ge(sem["scores_taken"], nth(b, "scores_taken", 16))
                    pe.wait_ge(sem["turn_taken"], nth(b, "turn_taken", 16))
                if half == 1 and kp == 0:
                    pe.wait_ge(sem["o_taken"], nth(b, "o_taken", 16))
                    pe.wait_ge(sem["state_ready"], nth(b, "state_ready", 16))
                    pe.wait_ge(sem["mean_taken"], nth(b, "mean_taken", A_HEADS))
                    pe.wait_ge(sem["p_exp"], nth(b, "p_exp", PAIRS))
                for j in range(2):
                    if j == 1:
                        mid()
                    for s in range(ROWS):
                        for step, (mx, wx) in enumerate(((mix_hi, w_hi), (mix_hi, w_lo), (mix_lo, w_hi))):
                            mm = nc.tensor.matmul(banks[4 * half + s][:], mx[:, 2 * kp + j, s * P:s * P + P],
                                                  wx[ws][:, j * 512:j * 512 + 512],
                                                  start=(kp == 0 and j == 0 and step == 0),
                                                  stop=(kp == 3 and j == 1 and step == 2))
                mm.then_inc(sem["unit_done"], 1)

            def v_turn(b, e):
                if e == 0:
                    pe.wait_ge(sem["proj_taken"], nth(b, "proj_taken", U_CV + 1))
                    pe.wait_ge(dve_ready, 2)
                    pe.wait_ge(sem["y_taken"], nth_before(b, "y_taken", 2 * ROWS))
                for p in range(PAIRS):
                    mm = nc.tensor.transpose(banks[2 + e][:, p * P:p * P + P], vt_[:, p * P + e * HD:p * P + e * HD + P], ident)
                mm.then_inc(sem["v_turned"], 1)

            def logits(b, p):
                for j in range(KV):
                    r = slice(j * HD, j * HD + HD)
                    for e in range(2):
                        at = p * P + e * HD
                        for g in range(2):
                            mm = nc.tensor.matmul(banks[6 + j][e * HD:e * HD + HD, g * P:g * P + P],
                                                  qt[g][r, at:at + HD], kt_[r, at:at + P], start=True, stop=True)
                mm.then_inc(sem["logits_done"], 1)

            def p_turn(b, p):
                pe.wait_ge(sem["p_ready"], nth(b, "p_ready", p + 1))
                if p:
                    pe.wait_ge(sem["pt_taken"], nth(b, "pt_taken", p))
                for h in range(4):
                    mm = nc.tensor.transpose(banks[4][:, h * P:h * P + P], prob[p % 2][:, h * P:h * P + P], ident)
                mm.then_inc(sem["p_turned"], 1)

            def attend(b, p):
                pe.wait_ge(sem["pt_taken"], nth(b, "pt_taken", p + 1))
                if p == 0:
                    pe.wait_ge(sem["v_taken"], nth(b, "v_taken", 2))
                else:
                    pe.wait_ge(sem["attend_taken"], nth(b, "attend_taken", p))
                pv = pt.rearrange("k (j g e t) -> k j g e t", j=2, g=2, e=2)
                ov = banks[5][:, 0:2 * P].rearrange("d (g e t) -> d g e t", g=2, e=2)
                for j in range(KV):
                    r = slice(j * HD, j * HD + HD)
                    for e in range(2):
                        mm = nc.tensor.matmul(ov[r, :, e, :], v_win[e][:, p * P + j * HD:p * P + j * HD + HD],
                                              pv[:, j, :, e, :], start=True, stop=True)
                mm.then_inc(sem["attend_done"], 1)

            def pool_mix(b, t):
                pe.wait_ge(sem["pooled"], nth(b, "pooled", t + 1))
                pe.wait_ge(sem["v_taken"], nth(b, "v_taken", t + 1))
                nc.tensor.matmul(banks[2 + t][:], pw[:, t, :], pooled[t][:], start=True, stop=True).then_inc(sem["pool_done"], 1)

            def chunk_scores(b, h, c):
                i = h * CHUNKS + c
                hb = heads[h % 2]
                t = slice(c * CHUNK, c * CHUNK + CHUNK)
                if c == 0:
                    pe.wait_ge(sem["prep_done"], nth(b, "prep_done", h + 1))
                    pe.wait_ge(sem["proj_taken"], nth(b, "proj_taken", U_HEAD[h] + 3))
                if i == 0:
                    pe.wait_ge(sem["pool_taken"], nth(b, "pool_taken", B_TILES))
                else:
                    pe.wait_ge(sem["turn_taken"], nth(b, "turn_taken", i))
                nc.tensor.transpose(banks[3][:, 0:P], hb[:, N_KEND, t], ident)
                nc.tensor.transpose(banks[3][:, P:2 * P], hb[:, N_V, t], ident).then_inc(sem["turned"], 1)
                if i:
                    pe.wait_ge(sem["scores_taken"], nth(b, "scores_taken", i))
                nc.tensor.matmul(banks[2][:, 0:P], hb[:, N_K8, t], hb[:, N_Q8, t], start=True, stop=True)
                for n, lv in enumerate(LEVELS):
                    upper = hb[:, N_L + n, t].rearrange("d (g two t) -> d g two t", two=2, t=lv)[:, :, 1, :]
                    mm = nc.tensor.matmul(banks[2][:, P + 64 * n:P + 64 * n + 64], hb[:, N_L + n, t], upper, start=True, stop=True)
                mm.then_inc(sem["scores_done"], 1)

            def chunk_out(b, h, c):
                i = h * CHUNKS + c
                hb = heads[h % 2]
                t = slice(c * CHUNK, c * CHUNK + CHUNK)
                pe.wait_ge(sem["turn_taken"], nth(b, "turn_taken", i + 1))
                pe.wait_ge(sem["scores_taken"], nth(b, "scores_taken", i + 1))
                if i == 0:
                    pe.wait_ge(sem["attend_taken"], nth(b, "attend_taken", PAIRS))
                else:
                    pe.wait_ge(sem["state_ready"], nth(b, "state_ready", i))
                    pe.wait_ge(sem["o_taken"], nth(b, "o_taken", i))
                kn, vn = kv_nat[i % 2][:, 0:P], kv_nat[i % 2][:, P:2 * P]
                nc.tensor.matmul(banks[5][:, 0:P], kn, vn, start=True, stop=True)
                nc.tensor.matmul(banks[4][:, 0:P], vn, sct[i % 2][:], start=True, stop=False)
                nc.tensor.matmul(banks[4][:, 0:P], state[:, h, :], hb[:, N_QIN, t], start=False, stop=True).then_inc(sem["chunk_done"], 1)

            def norm(b, h):
                pe.wait_ge(sem["o_taken"], nth(b, "o_taken", h * CHUNKS + CHUNKS))
                if h:
                    pe.wait_ge(sem["mean_taken"], nth(b, "mean_taken", h))
                nc.tensor.matmul(banks[6][:], mean_w, osq[h % 2][:], start=True, stop=True).then_inc(sem["mean_done"], 1)

            steps = {"v_turn": v_turn, "logits": logits, "p_turn": p_turn, "attend": attend, "pool_mix": pool_mix,
                     "chunk_scores": chunk_scores, "chunk_out": chunk_out, "norm": norm}

            def run(b, todo):
                for name, *at in todo:
                    if name in steps:
                        steps[name](b, *at)

            with pe.Fori(0, BLOCKS) as b:
                for n in range(UNITS):
                    (project if n < IN_UNITS else project_out)(b, n, lambda: run(b, S_TABLE[n][0]))
                    run(b, S_TABLE[n][1])

        @block.scalar
        def _(act):
            own = [0]

            def counted():
                own[0] += 1
                return 1

            act.dma_start(par[:], params).then_inc(params_in, 16)
            act.dma_start(kc[:], consts).then_inc(params_in, 16)
            act.preload_act_table_set("natural_log_exp_and_others")

            def high_x(j, src):
                j %= XP
                nc.scalar.activation(xt_hi[:, 2 * j:2 * j + 2, :], src[:].rearrange("p (a t) -> p a t", a=2),
                                     ACT.Copy).then_inc(sem["x_hi"], 1)

            def high_w(u, src):
                nc.scalar.activation(w_hi[w_slot(u)][:], src[:], ACT.Copy).then_inc(sem["w_hi"], 1)

            landed_count = [0, 0]

            def split_high(b, i, kind, n):
                landed_count[i % 2] += 1
                if b is None:
                    act.wait_ge(raw_in[i % 2], 16 * landed_count[i % 2])
                else:
                    act.wait_ge(raw_in[i % 2], b * (8 * len(BODY_PIECES)) + 16 * landed_count[i % 2])
                (high_x if kind == "x" else high_w)(n, raw[i % 2])

            for i, (kind, n) in enumerate(HEAD_PIECES):
                split_high(None, i, kind, n)
                if i == 0:
                    act.wait_ge(dve_ready, 1)
                    for g in range(4):
                        r = slice((g % 2) * HD, (g % 2) * HD + HD)
                        act.dma_start(pw[r, g // 2, r], pool_w[g]).then_inc(params_in, 16)
                    for dst, src in ((bout, b_out), (gain, ln_gain), (beta, ln_bias)):
                        act.dma_start(dst[:], src.partition_broadcast(P)).then_inc(params_in, 16)
                    nc.scalar.activation(lb_tmp[:, 1, :], lb_tmp[:, 0, :], ACT.Exp).then_inc(act_ready, 1)
            act.wait_ge(params_in, 16 * 9)
            act.wait_ge(dve_ready, 2)

            def bias(n):
                return par[:, PR_BIN + n:PR_BIN + n + 1]

            def take_unit(b, n):
                src = banks[n % 2][:]
                if n in CHAINS:
                    c = CHAINS.index(n)
                    if c >= 2:
                        name, count = used_event(CHAINS[c - 2])
                        act.wait_ge(sem[name], nth(b, name, count))
                    if n not in U_HEAD:
                        nc.scalar.activation(lin[c % 2][:], src, ACT.Identity, bias=bias(n))
                    nc.scalar.activation(sig[c % 2][:], src, ACT.Exp, bias=nbin[:, n:n + 1], scale=-1.0).then_inc(sem["proj_taken"], 1)
                    return
                if n < U_CK:
                    dst = qt[n - U_CQ]
                elif n == U_CK:
                    dst = kt_[:, HD:HD + TB]
                elif n == U_CV:
                    dst = vt_[:, HD:HD + TB]
                elif n < U_HEAD[0]:
                    dst = ub[:, n - U_B, PAD:PAD + TB]
                else:
                    h = U_HEAD.index(n - 2)
                    dst = heads[h % 2][:, N_V, :]
                    if h == 1:
                        act.wait_ge(sem["attend_done"], nth(b, "attend_done", PAIRS))
                    elif h >= 2:
                        act.wait_ge(sem["chunk_done"], nth(b, "chunk_done", 4 * (h - 1)))
                nc.scalar.activation(dst, src, ACT.Identity, bias=bias(n)).then_inc(sem["proj_taken"], 1)

            def sigmoid(b, c):
                act.wait_ge(sem["d_ready"], nth(b, "d_ready", c + 1))
                nc.scalar.activation(sig[c % 2][:], sig[c % 2][:], ACT.Ln).then_inc(act_step, counted())
                act.wait_ge(act_step, own[0])
                nc.scalar.activation(sig[c % 2][:], sig[c % 2][:], ACT.Exp, scale=-1.0).then_inc(sem["sig_ready"], 1)

            def v_turn(b, e):
                act.wait_ge(sem["v_turned"], nth(b, "v_turned", e + 1))
                nc.scalar.activation(v_win[e], banks[2 + e][:], ACT.Copy).then_inc(sem["v_taken"], 1)

            def logits(b, p):
                act.wait_ge(sem["max_ready"], nth(b, "max_ready", p + 1))
                for h in range(4):
                    j, g = divmod(h, 2)
                    nc.scalar.activation(prob[p % 2][:, h * P:h * P + P], banks[6 + j][:, g * P:g * P + P], ACT.Exp,
                                         bias=nm[:, p % 2, h:h + 1], scale=SCALE, accum_out=den[:, p % 2, h:h + 1])
                ins = nc.scalar.activation(es[:, p % 2, :], es[:, p % 2, :], ACT.Exp)
                ins.then_inc(sem["p_exp"], 1)

            def p_turn(b, p):
                act.wait_ge(sem["p_turned"], nth(b, "p_turned", p + 1))
                if p:
                    act.wait_ge(sem["attend_done"], nth(b, "attend_done", p))
                nc.scalar.activation(pt, banks[4][:], ACT.Copy).then_inc(sem["pt_taken"], 1)

            def attend(b, p):
                act.wait_ge(sem["attend_done"], nth(b, "attend_done", p + 1))
                nc.scalar.activation(mixed[:, M_C:M_C + 2, p * P:p * P + P], banks[5][:, 0:2 * P].rearrange("d (g t) -> d g t", g=2),
                                     ACT.Copy).then_inc(sem["attend_taken"], 1)
                if p == PAIRS - 1:
                    for buf in (kt_, vt_):
                        ins = nc.scalar.activation(buf[:, 0:HD], buf[:, TB:TB + HD], ACT.Copy)
                    ins.then_inc(sem["carry_done"], 1)

            def pool_mix(b, t):
                act.wait_ge(sem["pool_done"], nth(b, "pool_done", t + 1))
                nc.scalar.activation(mixed[:, M_B + t, :], banks[2 + t][:], ACT.Copy,
                                     scale=par[:, PR_PSC + t:PR_PSC + t + 1]).then_inc(sem["pool_taken"], 1)

            def log_decay(b, h):
                act.wait_ge(sem["floored"], nth(b, "floored", h + 1))
                nc.scalar.activation(logf[:], logf[:], ACT.Ln).then_inc(sem["logf_ready"], 1)

            def exponentials(b, h):
                hb = heads[h % 2]
                base = 6 * h
                act.wait_ge(sem["diff_ready"], nth(b, "diff_ready", base + 1))
                nc.scalar.activation(hb[:, N_Q8, :], hb[:, N_K8, :], ACT.Exp)
                nc.scalar.activation(hb[:, N_EIN, :], b128[:], ACT.Exp)
                nc.scalar.activation(hb[:, N_K8, :], hb[:, N_K8, :], ACT.Exp, scale=-1.0).then_inc(sem["exp_ready"], 1)
                for n, lv in enumerate(LEVELS):
                    act.wait_ge(sem["diff_ready"], nth(b, "diff_ready", base + 2 + n))
                    v = hb[:, N_L + n, :].rearrange("d (g two t) -> d g two t", two=2, t=lv)
                    up = b16[:].rearrange("d (g two t) -> d g two t", two=2, t=lv) if lv == 16 else v
                    nc.scalar.activation(v[:, :, 0, :], v[:, :, 0, :], ACT.Exp, scale=-1.0)
                    nc.scalar.activation(v[:, :, 1, :], up[:, :, 1, :], ACT.Exp).then_inc(sem["exp_ready"], 1)
                act.wait_ge(sem["diff_ready"], nth(b, "diff_ready", base + 6))
                nc.scalar.activation(hb[:, N_KEND, :], hb[:, N_KEND, :], ACT.Exp, scale=-1.0).then_inc(sem["exp_ready"], 1)

            def chunk_scores(b, h, c):
                i = h * CHUNKS + c
                act.wait_ge(sem["turned"], nth(b, "turned", i + 1))
                if i >= 2:
                    act.wait_ge(sem["chunk_done"], nth(b, "chunk_done", i - 1))
                nc.scalar.activation(kv_nat[i % 2][:], banks[3][:, 0:2 * P], ACT.Copy).then_inc(sem["turn_taken"], 1)

            def chunk_out(b, h, c):
                i = h * CHUNKS + c
                t = slice(c * CHUNK, c * CHUNK + CHUNK)
                act.wait_ge(sem["chunk_done"], nth(b, "chunk_done", i + 1))
                if h >= 2 and c == 0:
                    act.wait_ge(sem["mean_done"], nth(b, "mean_done", h - 1))
                    act.wait_ge(sem["norm_done"], nth(b, "norm_done", h - 1))
                nc.scalar.activation(mixed[:, M_A + h, t], banks[4][:, 0:P], ACT.Copy)
                nc.scalar.activation(osq[h % 2][:, t], banks[4][:, 0:P], ACT.Square).then_inc(sem["o_taken"], 1)

            def norm(b, h):
                act.wait_ge(sem["mean_done"], nth(b, "mean_done", h + 1))
                nc.scalar.activation(osq[h % 2][:], banks[6][:], ACT.Ln, bias=eps[:]).then_inc(sem["mean_taken"], 1)
                act.wait_ge(sem["mean_taken"], nth(b, "mean_taken", h + 1))
                nc.scalar.activation(osq[h % 2][:], osq[h % 2][:], ACT.Exp, scale=-0.5).then_inc(sem["inv_ready"], 1)

            steps = {"v_turn": v_turn, "logits": logits, "p_turn": p_turn, "attend": attend, "pool_mix": pool_mix, "sigmoid": sigmoid,
                     "log_decay": log_decay, "exponentials": exponentials, "chunk_scores": chunk_scores, "chunk_out": chunk_out, "norm": norm}

            def run(b, todo):
                for name, *at in todo:
                    if name in steps:
                        steps[name](b, *at)

            with act.Fori(0, BLOCKS) as b:
                i = len(HEAD_PIECES)
                for n in range(UNITS):
                    run(b, S_TABLE[n][0])
                    act.wait_ge(sem["unit_done"], nth(b, "unit_done", n + 1))
                    if n < IN_UNITS:
                        take_unit(b, n)
                    for piece in SPLITS[n]:
                        split_high(b, i, *piece)
                        i += 1
                    run(b, S_TABLE[n][1])
                act.wait_ge(sem["var_ready"], nth(b, "var_ready", 1))
                nc.scalar.activation(rstd[:], mv[:, :, 1], ACT.Ln, bias=eps[:]).then_inc(act_step, counted())
                act.wait_ge(act_step, own[0])
                nc.scalar.activation(rstd[:], rstd[:], ACT.Exp, scale=-0.5).then_inc(sem["rstd_ready"], 1)
                act.wait_ge(sem["nmr_ready"], nth(b, "nmr_ready", 1))
                for s in range(ROWS):
                    nc.scalar.activation(rows[:, s, :], rows[:, s, :], ACT.Identity, bias=nmr[:, s:s + 1],
                                         scale=rstd[:, s:s + 1]).then_inc(sem["normed"], 1)
                act.sem_clear(act_step)
                own[0] = 0

        @block.vector
        def _(dve):
            own = [0]

            def counted():
                own[0] += 1
                return 1

            dve.sem_inc(sem["y_taken"], PER["y_taken"])
            dve.wait_ge(params_in, 16 * 2)
            logit = par[:, PR_LB:PR_LB + A_HEADS]
            nc.vector.memset(pw[:], 0.0).then_inc(dve_step, counted())
            dve.wait_ge(dve_step, own[0])
            nc.vector.tensor_tensor(lb_tmp[:, 0, :], logit, logit, ALU.subtract).then_inc(dve_ready, 1)

            def split_low(b, i, kind, n):
                if b is None:
                    dve.wait_ge(sem[f"{kind}_hi"], n + 1)
                else:
                    dve.wait_ge(sem[f"{kind}_hi"], nth(b, f"{kind}_hi", n + 1))
                src = raw[i % 2][:]
                if kind == "w":
                    nc.vector.tensor_tensor(w_lo[w_slot(n)][:], src, w_hi[w_slot(n)][:].bitcast(F32), ALU.subtract).then_inc(sem["w_lo"], 1)
                else:
                    pair = slice(2 * (n % XP), 2 * (n % XP) + 2)
                    nc.vector.tensor_tensor(xt_lo[:, pair, :], src.rearrange("p (a t) -> p a t", a=2),
                                            xt_hi[:, pair, :].bitcast(F32), ALU.subtract).then_inc(sem["x_lo"], 1)

            for i, (kind, n) in enumerate(HEAD_PIECES):
                split_low(None, i, kind, n)
            for buf in (state, sct[0], sct[1], kt_, vt_, ub):
                nc.vector.memset(buf[:], 0.0).then_inc(dve_step, counted())
            nc.vector.memset(eps[:], EPS).then_inc(dve_step, counted())
            nc.vector.tensor_scalar(nbin[:], par[:, PR_BIN:PR_BIN + IN_UNITS], -1.0, None, ALU.mult).then_inc(dve_step, counted())
            nc.vector.tensor_scalar(nsink[:], par[:, PR_SINK:PR_SINK + 4], -1.0, None, ALU.mult).then_inc(dve_step, counted())
            dve.wait_ge(act_ready, 1)
            nc.vector.reciprocal(lb_tmp[:, 2, :], lb_tmp[:, 1, :]).then_inc(dve_step, counted())
            dve.wait_ge(dve_step, own[0])
            nc.vector.tensor_tensor(lb_tmp[:, 2, :], lb_tmp[:, 1, :], lb_tmp[:, 2, :], ALU.mult).then_inc(dve_step, counted())
            dve.wait_ge(dve_step, own[0])
            nc.vector.tensor_tensor(lb[:], lb_tmp[:, 2, :], lb_tmp[:, 2, :], ALU.subtract).then_inc(dve_step, counted())
            dve.wait_ge(dve_step, own[0])
            nc.vector.tensor_scalar(lb[:], lb[:], 0.0, None, ALU.max).then_inc(dve_step, counted())
            dve.wait_ge(dve_step, own[0])
            nc.vector.tensor_scalar(one_lb[:], lb[:], -1.0, 1.0, ALU.mult, ALU.add).then_inc(dve_ready, 1)
            dve.wait_ge(dve_ready, 2)
            dve.sem_clear(dve_step)
            own[0] = 0

            def start_sigmoid(b, c):
                dve.wait_ge(sem["proj_taken"], nth(b, "proj_taken", CHAINS[c] + 1))
                nc.vector.tensor_scalar(sig[c % 2][:], sig[c % 2][:], EXP_CAP, 1.0, ALU.min, ALU.add).then_inc(sem["d_ready"], 1)

            def use_sigmoid(b, c):
                n = CHAINS[c]
                dve.wait_ge(sem["sig_ready"], nth(b, "sig_ready", c + 1))
                s, x = sig[c % 2][:], lin[c % 2][:]
                if n in U_GATE:
                    m = U_GATE.index(n)
                    if m < M_B:
                        dve.wait_ge(sem["attend_taken"], nth(b, "attend_taken", PAIRS))
                    elif m < M_A:
                        dve.wait_ge(sem["pool_taken"], nth(b, "pool_taken", B_TILES))
                    nc.vector.tensor_tensor(s, s, x, ALU.mult).then_inc(dve_step, counted())
                    dve.wait_ge(dve_step, own[0])
                    nc.vector.tensor_tensor(s, s, mixed[:, m, :], ALU.mult).then_inc(dve_step, counted())
                    dve.wait_ge(dve_step, own[0])
                    nc.vector.tensor_copy(mix_hi[:, m, :], s).then_inc(dve_step, counted())
                    dve.wait_ge(dve_step, own[0])
                    nc.vector.tensor_tensor(mix_lo[:, m, :], s, mix_hi[:, m, :].bitcast(F32), ALU.subtract).then_inc(sem["mix_ready"], 1)
                    return
                if n in U_HEAD:
                    h = U_HEAD.index(n)
                    nc.vector.tensor_scalar(s, s, one_lb[:, h:h + 1], lb[:, h:h + 1], ALU.mult, ALU.add).then_inc(dve_step, counted())
                    dve.wait_ge(dve_step, own[0])
                    nc.vector.tensor_scalar(logf[:], s, F_FLOOR, None, ALU.max).then_inc(sem["floored"], 1)
                    nc.vector.tensor_scalar(k[:], s, -1.0, 1.0, ALU.mult, ALU.add).then_inc(sem["sig_used"], 1)
                else:
                    nc.vector.tensor_tensor(q[:], x, s, ALU.mult).then_inc(sem["sig_used"], 1)

            def windows(b, t):
                dve.wait_ge(sem["proj_taken"], nth(b, "proj_taken", U_B + t + 1))
                n = PAD + TB
                lo_, hi_ = slice(0, HD), slice(HD, P)
                a, c = win
                u = ub[:, t, :]
                nc.vector.tensor_tensor(a[:, 1:n], u[:, 1:n], u[:, 0:n - 1], ALU.add).then_inc(dve_step, counted())
                dve.wait_ge(dve_step, own[0])
                r = hi_ if t == 0 else slice(0, P)
                nc.vector.tensor_tensor(c[r, 3:n], a[r, 3:n], a[r, 1:n - 2], ALU.add).then_inc(dve_step, counted())
                dve.wait_ge(dve_step, own[0])
                if t == 1:
                    nc.vector.tensor_tensor(a[:, 7:n], c[:, 7:n], c[:, 3:n - 4], ALU.add).then_inc(dve_step, counted())
                    dve.wait_ge(dve_step, own[0])
                    nc.vector.tensor_tensor(c[hi_, 15:n], a[hi_, 15:n], a[hi_, 7:n - 8], ALU.add).then_inc(dve_step, counted())
                    dve.wait_ge(dve_step, own[0])
                for r, s in ((lo_, a), (hi_, c)):
                    nc.vector.tensor_tensor(s[r, PAD:2 * PAD], s[r, PAD:2 * PAD],
                                                 kc[r, K_CORR + t * PAD:K_CORR + (t + 1) * PAD], ALU.mult).then_inc(dve_step, counted())
                dve.wait_ge(dve_step, own[0])
                for r, s in ((lo_, a), (hi_, c)):
                    ins = nc.vector.scalar_tensor_tensor(out=pooled[t][r, :], in0=s[r, PAD:n], scalar=kc[r, K_WINV + t:K_WINV + t + 1],
                                                         in1=u[r, PAD:n], op0=ALU.mult, op1=ALU.subtract)
                    if r is lo_:
                        ins.then_inc(dve_step, counted())
                ins.then_inc(sem["pooled"], 1)
                dve.wait_ge(sem["pooled"], nth(b, "pooled", t + 1))
                nc.vector.tensor_copy(ub[:, t, 0:PAD], ub[:, t, TB:TB + PAD])
                nc.vector.memset(kc[:, K_CORR + t * PAD:K_CORR + (t + 1) * PAD], 1.0)

            def logits(b, p):
                dve.wait_ge(sem["logits_done"], nth(b, "logits_done", p + 1))
                if p == 0:
                    for j in range(KV):
                        v = banks[6 + j][:, 0:2 * P].rearrange("q (g s) -> q g s", g=2)
                        nc.vector.tensor_tensor(v, v, kc[:, K_PEN:K_PEN + P].unsqueeze(1).broadcast_to([P, 2, P]), ALU.add).then_inc(dve_step, counted())
                    dve.wait_ge(dve_step, own[0])
                    nc.vector.memset(kc[:, K_PEN:K_PEN + P], 0.0).then_inc(dve_step, counted())
                for j in range(KV):
                    nc.vector.tensor_reduce(cmax[:, p % 2, 2 * j:2 * j + 2],
                                                 banks[6 + j][:, 0:2 * P].rearrange("q (g s) -> q g s", g=2), AX.X, ALU.max).then_inc(dve_step, counted())
                dve.wait_ge(dve_step, own[0])
                nc.vector.scalar_tensor_tensor(out=nm[:, p % 2, :], in0=cmax[:, p % 2, :], scalar=-SCALE, in1=nsink[:],
                                                    op0=ALU.mult, op1=ALU.min).then_inc(dve_step, counted())
                dve.wait_ge(dve_step, own[0])
                nc.vector.tensor_tensor(es[:, p % 2, :], nm[:, p % 2, :], nsink[:], ALU.subtract).then_inc(sem["max_ready"], 1)

            def normalise(b, p):
                dve.wait_ge(sem["p_exp"], nth(b, "p_exp", p + 1))
                nc.vector.tensor_tensor(den[:, p % 2, :], den[:, p % 2, :], es[:, p % 2, :], ALU.add).then_inc(dve_step, counted())
                dve.wait_ge(dve_step, own[0])
                nc.vector.reciprocal(rden[:, p % 2, :], den[:, p % 2, :]).then_inc(dve_step, counted())
                dve.wait_ge(dve_step, own[0])
                v = prob[p % 2].rearrange("q (h s) -> q h s", h=4)
                nc.vector.tensor_tensor(v, v, rden[:, p % 2, :].unsqueeze(2).broadcast_to([P, 4, P]), ALU.mult).then_inc(sem["p_ready"], 1)

            def differences(b, h):
                hb = heads[h % 2]
                dve.wait_ge(sem["logf_ready"], nth(b, "logf_ready", h + 1))
                if h == 0:
                    dve.wait_ge(sem["out_landed"], nth_before(b, "out_landed", 16 * ROWS))
                if h == 1:
                    dve.wait_ge(sem["attend_done"], nth(b, "attend_done", PAIRS))
                if h >= 2:
                    dve.wait_ge(sem["chunk_done"], nth(b, "chunk_done", 4 * (h - 1)))
                nc.vector.tensor_tensor_scan(b16[:], kc[:, K_R16:K_R16 + TB], logf[:], 0.0, ALU.mult, ALU.add).then_inc(dve_step, counted())
                dve.wait_ge(dve_step, own[0])
                nc.vector.tensor_tensor_scan(b128[:], kc[:, K_R128:K_R128 + TB], logf[:], 0.0, ALU.mult, ALU.add).then_inc(dve_step, counted())
                dve.wait_ge(dve_step, own[0])

                def minus(dst, src, seg, at, n=None):
                    n = n or seg
                    v = src[:].rearrange("d (g t) -> d g t", t=seg)
                    return nc.vector.tensor_tensor(dst.rearrange("d (g t) -> d g t", t=seg)[:, :, 0:n], v[:, :, 0:n],
                                                   v[:, :, at:at + 1].broadcast_to([P, TB // seg, n]), ALU.subtract)

                minus(hb[:, N_K8, :], b16, 8, 3).then_inc(sem["diff_ready"], 1)
                for n, lv in enumerate(LEVELS):
                    minus(hb[:, N_L + n, :], b16 if lv <= 16 else b128, 2 * lv, lv - 1,
                          lv if lv == 16 else None).then_inc(sem["diff_ready"], 1)
                minus(hb[:, N_KEND, :], b128, CHUNK, CHUNK - 1).then_inc(sem["diff_ready"], 1)

            def products(b, h):
                hb = heads[h % 2]
                base = 6 * h
                dve.wait_ge(sem["exp_ready"], nth(b, "exp_ready", base + 1))
                nc.vector.tensor_tensor(hb[:, N_Q8, :], hb[:, N_Q8, :], q[:], ALU.mult).then_inc(dve_step, counted())
                nc.vector.tensor_tensor(hb[:, N_K8, :], hb[:, N_K8, :], k[:], ALU.mult).then_inc(dve_step, counted())
                nc.vector.tensor_tensor(hb[:, N_QIN, :], hb[:, N_EIN, :], q[:], ALU.mult).then_inc(dve_step, counted())
                for n, lv in enumerate(LEVELS):
                    dve.wait_ge(sem["exp_ready"], nth(b, "exp_ready", base + 2 + n))
                    for half, src in enumerate((k, q)):
                        v = hb[:, N_L + n, :].rearrange("d (g two t) -> d g two t", two=2, t=lv)[:, :, half, :]
                        sv = src[:].rearrange("d (g two t) -> d g two t", two=2, t=lv)[:, :, half, :]
                        nc.vector.tensor_tensor(v, v, sv, ALU.mult).then_inc(dve_step, counted())
                dve.wait_ge(sem["exp_ready"], nth(b, "exp_ready", base + 6))
                nc.vector.tensor_tensor(hb[:, N_KEND, :], hb[:, N_KEND, :], k[:], ALU.mult).then_inc(sem["prep_done"], 1)

            def chunk_scores(b, h, c):
                i = h * CHUNKS + c
                dve.wait_ge(sem["scores_done"], nth(b, "scores_done", i + 1))
                if i >= 2:
                    dve.wait_ge(sem["chunk_done"], nth(b, "chunk_done", i - 1))
                nc.vector.tensor_copy(sct[i % 2][0:64, 64:P], banks[2][0:64, P + 192:P + 256]).then_inc(dve_step, counted())
                dve.wait_ge(dve_step, own[0])
                nc.vector.copy_predicated(sct[i % 2][:], masks[:, 0:P], banks[2][:, 0:P]).then_inc(dve_step, counted())
                dve.wait_ge(dve_step, own[0])
                for n, lv in enumerate(LEVELS[:-1]):
                    cols = slice(P + 64 * n, P + 64 * n + 64)
                    dst = sct[i % 2][:].rearrange("s (g two t) -> s g two t", two=2, t=lv)[:, :, 1, :]
                    ins = nc.vector.copy_predicated(dst, masks[:, cols].rearrange("s (g t) -> s g t", t=lv),
                                                    banks[2][:, cols].rearrange("s (g t) -> s g t", t=lv))
                    if n < 2:
                        ins.then_inc(dve_step, counted())
                        dve.wait_ge(dve_step, own[0])
                ins.then_inc(sem["scores_taken"], 1)

            def chunk_out(b, h, c):
                i = h * CHUNKS + c
                dve.wait_ge(sem["chunk_done"], nth(b, "chunk_done", i + 1))
                last = c * CHUNK + CHUNK - 1
                nc.vector.scalar_tensor_tensor(out=state[:, h, :], in0=state[:, h, :], scalar=heads[h % 2][:, N_EIN, last:last + 1],
                                               in1=banks[5][:, 0:P], op0=ALU.mult, op1=ALU.add).then_inc(sem["state_ready"], 1)

            def norm(b, h):
                dve.wait_ge(sem["inv_ready"], nth(b, "inv_ready", h + 1))
                m = mixed[:, M_A + h, :]
                nc.vector.scalar_tensor_tensor(out=m, in0=m, scalar=par[:, PR_GAIN + h:PR_GAIN + h + 1], in1=osq[h % 2][:],
                                               op0=ALU.mult, op1=ALU.mult).then_inc(sem["norm_done"], 1)

            def residual(b, s):
                dve.wait_ge(sem["x_in"], nth(b, "x_in", 16 * ROWS))
                nc.vector.scalar_tensor_tensor(out=rows[:, s, :], in0=rows[:, s, :], scalar=ALPHA, in1=bout[:],
                                                    op0=ALU.mult, op1=ALU.add).then_inc(dve_step, counted())

            def take_rows(b, half):
                dve.wait_ge(sem["unit_done"], nth(b, "unit_done", IN_UNITS + 4 * half + 4))
                cols = slice(512 * half, 512 * half + 512)
                if half == 0:
                    dve.wait_ge(dve_step, own[0])
                for s in range(ROWS):
                    r = rows[:, s, cols]
                    nc.vector.tensor_tensor(r, banks[4 * half + s][:], r, ALU.add).then_inc(sem["y_taken"], 1)
                for s in range(ROWS):
                    dve.wait_ge(sem["y_taken"], nth(b, "y_taken", 4 * half + s + 1))
                    nc.vector.bn_stats(stats[:, s, half, :], rows[:, s, cols]).then_inc(dve_step, counted())

            steps = {"windows": windows, "logits": logits, "normalise": normalise, "differences": differences, "products": products,
                     "use_sigmoid": use_sigmoid, "chunk_scores": chunk_scores, "chunk_out": chunk_out, "norm": norm,
                     "residual": residual, "take_rows": take_rows}

            def run(b, todo):
                for name, *at in todo:
                    if name in steps:
                        steps[name](b, *at)

            with dve.Fori(0, BLOCKS) as b:
                i = len(HEAD_PIECES)
                for n in range(UNITS):
                    run(b, S_TABLE[n][0])
                    if n in CHAINS:
                        start_sigmoid(b, CHAINS.index(n))
                    for piece in SPLITS[n]:
                        split_low(b, i, *piece)
                        i += 1
                    run(b, S_TABLE[n][1])
                dve.wait_ge(dve_step, own[0])
                for s in range(ROWS):
                    nc.vector.bn_aggr(mv[:, s, :], stats[:, s, :, :].rearrange("p a c -> p (a c)")).then_inc(dve_step, counted())
                dve.wait_ge(dve_step, own[0])
                nc.vector.tensor_scalar(nmr[:], mv[:, :, 0], -1.0, None, ALU.mult).then_inc(sem["var_ready"], 1)
                dve.wait_ge(sem["rstd_ready"], nth(b, "rstd_ready", 1))
                nc.vector.tensor_tensor(nmr[:], nmr[:], rstd[:], ALU.mult).then_inc(sem["nmr_ready"], 1)
                for s in range(ROWS):
                    dve.wait_ge(sem["normed"], nth(b, "normed", s + 1))
                    nc.vector.tensor_tensor(rows[:, s, :], rows[:, s, :], gain[:], ALU.mult).then_inc(sem["scaled"], 1)
                dve.sem_clear(dve_step)
                own[0] = 0


def kernel(x, w_in, b_in, lb_logits, a_norm_gain, pool_w, pool_scale, attn_sinks, w_out, b_out, ln_gain, ln_bias):
    import concourse.bacc as _bacc
    from concourse.bass_utils import run_bass_kernel_spmd as _run

    x, w_in, w_out = np.asarray(x)[0], np.asarray(w_in)[0], np.asarray(w_out)[0]
    xt = x.reshape(BLOCKS, TB, XP, 2, P).transpose(0, 2, 4, 3, 1).reshape(BLOCKS, XP, P, 2 * TB)
    xt = np.concatenate([xt, xt[:1]])
    xr = x.reshape(BLOCKS, ROWS, P, D)
    cols = column_order()
    w_units = [w_in[:, c].reshape(KT, P, P).transpose(1, 0, 2).reshape(P, KT * P) for c in cols]
    wo = w_out[np.concatenate(mixing_order())].reshape(4, 2, P, 2, 512)
    w_units += [wo[kp, :, :, half].transpose(1, 0, 2).reshape(P, 1024) for half in range(2) for kp in range(4)]
    params = np.concatenate([
        np.asarray(b_in)[0][np.stack(cols)].T,
        np.asarray(lb_logits)[0].reshape(A_HEADS, P).T,
        np.asarray(a_norm_gain)[0].reshape(A_HEADS, P).T,
        np.asarray(pool_scale)[0].reshape(B_TILES, P).T,
        np.broadcast_to(np.asarray(attn_sinks)[0][None, :], (P, 4)),
    ], axis=1)
    arrays = {"xt": xt, "xr": xr, "w": np.stack(w_units), "params": params, "consts": constants(),
              "pool_w": np.asarray(pool_w)[0], "b_out": np.asarray(b_out)[0], "ln_gain": np.asarray(ln_gain)[0],
              "ln_bias": np.asarray(ln_bias)[0]}
    arrays = {name: np.ascontiguousarray(a) for name, a in arrays.items()}
    nc = _bacc.Bacc("TRN2", target_bir_lowering=False, num_devices=1)
    args = [nc.dram_tensor(name, a.shape, mybir.dt.from_np(a.dtype), kind="ExternalInput").ap() for name, a in arrays.items()]
    out = nc.dram_tensor("out", (BLOCKS, ROWS, P, D), F32, kind="ExternalOutput").ap()
    trunk_kernel(nc, *args, out)
    r = _run(nc, [arrays], core_ids=[0])
    return r.results[0]["out"].reshape(1, SEQ, D)
```

```python
from contextlib import ExitStack

import numpy as np

import concourse.bass as bass
from concourse import mybir

F32 = mybir.dt.float32
F32R = mybir.dt.float32r
I32 = mybir.dt.int32
ALU = mybir.AluOpType
ACT = mybir.ActivationFunctionType
AX = mybir.AxisListType

P = 128
D = 1024
SEQ = 2048
TB = 512
BLOCKS = SEQ // TB
KT = D // P
A_HEADS, B_TILES, KV = 4, 2, 2
HD = 64
EPS = 1e-5
F_FLOOR = 1e-6
NEG = -1e30
ALPHA = 2.0 ** 0.25
SCALE = HD ** -0.5
EXP_CAP = 2.0 ** 60
POOL_WINDOWS = (2, 4, 8, 16)
PAD = 16
CHUNK = 128
CHUNKS = TB // CHUNK
PAIRS = TB // P
LEVELS = (8, 16, 32, 64)

IN_UNITS = 26
OUT_UNITS = 8
UNITS = IN_UNITS + OUT_UNITS
XP = KT // 2
ROWS = TB // P

U_CQ, U_CK, U_CV = 0, 2, 3
U_B = (4, 8)
U_HEAD = (5, 9, 13, 17)
U_LOGITS = 3
U_GATE = (12, 16, 20, 21, 22, 23, 24, 25)
CHAINS = tuple(sorted(U_GATE + U_HEAD + tuple(u + 1 for u in U_HEAD)))
M_C, M_B, M_A = 0, 2, 4

PR_BIN, PR_LB, PR_GAIN, PR_PSC, PR_SINK = 0, 26, 30, 34, 36
PR_N = 40
K_ID, K_MEAN, K_R16, K_R128, K_PEN, K_CORR, K_WINV, K_UP, K_MASK = 0, 128, 256, 768, 1280, 1408, 1440, 1442, 1443
K_N = K_MASK + 128 + 4 * 64


def column_order():
    a, b, c, kv = 512, 256, 256, 128
    q0, f0, i0 = 0, a, 2 * a
    u0 = 3 * a
    c0 = u0 + b
    k0, v0, z0 = c0 + c, c0 + c + kv, c0 + c + 2 * kv

    def heads(base, g):
        return np.concatenate([base + (j * 2 + g) * HD + np.arange(HD) for j in range(KV)])

    tiles = [heads(c0, 0), heads(c0, 1), k0 + np.arange(P), v0 + np.arange(P)]
    tiles += [None] * (IN_UNITS - len(tiles))
    for t, u in enumerate(U_B):
        tiles[u] = u0 + t * P + np.arange(P)
    for h, u in enumerate(U_HEAD):
        tiles[u:u + 3] = [base + h * P + np.arange(P) for base in (f0, q0, i0)]
    for u, m in zip(U_GATE, mixing_order()):
        tiles[u] = z0 + m
    return tiles


def mixing_order():
    tiles = [2 * 256 + 256 + np.concatenate([(j * 2 + g) * HD + np.arange(HD) for j in range(KV)]) for g in range(2)]
    tiles += [512 + t * P + np.arange(P) for t in range(B_TILES)]
    return tiles + [h * P + np.arange(P) for h in range(A_HEADS)]


def constants():
    k = np.zeros((P, K_N), np.float32)
    t = np.arange(TB)
    k[:, K_ID:K_ID + P] = np.eye(P)
    k[:, K_MEAN:K_MEAN + P] = 1.0 / P
    k[:, K_R16:K_R16 + TB] = t % 16 != 0
    k[:, K_R128:K_R128 + TB] = t % CHUNK != 0
    k[:, K_PEN:K_PEN + HD] = NEG
    k[HD:P, K_UP] = 1.0
    for g, w in enumerate(POOL_WINDOWS):
        rows = slice((g % 2) * HD, (g % 2) * HD + HD)
        k[rows, K_CORR + (g // 2) * PAD:K_CORR + (g // 2 + 1) * PAD] = w / np.minimum(np.arange(PAD) + 1, w)
        k[rows, K_WINV + g // 2] = 1.0 / w
    s, tt = np.arange(P)[:, None], np.arange(P)[None, :]
    k[:, K_MASK:K_MASK + P] = (s // 8 == tt // 8) & (s <= tt)
    for n, lv in enumerate(LEVELS):
        upper = (tt // lv % 2 == 1)[0]
        m = (s // (2 * lv) == tt // (2 * lv)) & (s // lv % 2 == 0)
        k[:, K_MASK + P + 64 * n:K_MASK + P + 64 * (n + 1)] = m[:, upper]
    return k


def schedule():
    table = [([], []) for _ in range(UNITS)]
    MID, AFTER = 0, 1

    def put(n, half, *step):
        table[n][half].append(step)

    for h, u in enumerate(U_HEAD):
        put(u + 9, AFTER, "norm", h)
    for h, u in enumerate(U_HEAD):
        for c in range(CHUNKS):
            put(u + 5 + c, MID, "chunk_scores", h, c)
            put(u + 5 + c, AFTER, "chunk_out", h, c)
        put(u + 9, MID, "split_squares", h)
    put(U_CV + 1, MID, "v_turn", 0)
    put(U_CV + 1, AFTER, "v_turn", 1)
    for p in range(PAIRS):
        put(U_LOGITS + 3 + p, MID, "attend", p)
    for p in range(PAIRS):
        put(U_LOGITS + 1 + p, MID, "normalise", p)
        put(U_LOGITS + 2 + p, MID, "p_turn", p)
    for p in range(PAIRS):
        put(U_LOGITS + p, AFTER, "logits", p)
    put(U_B[0] + 1, AFTER, "windows", 0)
    put(U_B[0] + 5, MID, "pool_mix", 0)
    put(U_B[1] + 2, MID, "windows", 1)
    put(U_B[1] + 4, MID, "pool_mix", 1)
    for h, u in enumerate(U_HEAD):
        put(u + 4, MID, "products", h, 1)
    for c, u in enumerate(CHAINS):
        put(u + 1, MID, "sigmoid", c)
        put(u + (2 if u == U_GATE[-1] else 1), MID, "use_sigmoid", c)
    for h, u in enumerate(U_HEAD):
        put(u + 1, AFTER, "log_decay", h)
        put(u + 2, MID, "differences", h)
        put(u + 2, AFTER, "exponentials", h, 0)
        put(u + 3, MID, "exponentials", h, 1)
        put(u + 3, MID, "products", h, 0)
    for s in range(ROWS):
        put(25 + s, AFTER, "residual", s)
    put(IN_UNITS + 3, AFTER, "take_rows", 0)
    return table


def unit_bank(n):
    return n if n < 4 else n % 2


def w_slot(u):
    u %= UNITS
    return 1 if u == UNITS - 1 else u % 3


HEAD_PIECES = [("w", n) for n in range(5)]
SPLITS = [[], []] + [[("w", n + 3)] for n in range(2, IN_UNITS)]
SPLITS += [[("x", XP + j), ("w", IN_UNITS + 3 + j)] for j in range(XP)]
SPLITS += [[], [("w", 33)], [("w", 34)], []]
IN_NEXT = [("w", UNITS + 1), ("w", UNITS + 2), ("w", UNITS + 3), ("w", UNITS + 4)]
BODY_PIECES = [p for after in SPLITS for p in after] + IN_NEXT
AHEAD_LOADS = 1


PER = {
    "unit_done": UNITS, "w_hi": UNITS, "w_lo": UNITS, "x_hi": XP, "x_lo": XP,
    "proj_taken": IN_UNITS, "d_ready": 16, "sig_ready": 16, "sig_used": 8,
    "floored": A_HEADS, "logf_ready": A_HEADS, "diff_ready": 6 * A_HEADS, "exp_ready": 6 * A_HEADS,
    "prep_done": A_HEADS, "turned": 16, "scores_done": 16, "turn_taken": 16, "scores_taken": 16,
    "chunk_done": 16, "o_taken": 16, "state_ready": 16, "mean_done": A_HEADS, "mean_taken": A_HEADS, "squares_split": A_HEADS,
    "inv_ready": A_HEADS, "norm_done": A_HEADS,
    "v_turned": 2, "v_taken": 2, "logits_done": PAIRS, "max_ready": PAIRS, "p_exp": PAIRS, "p_ready": PAIRS,
    "p_turned": PAIRS, "pt_taken": PAIRS, "attend_done": PAIRS, "attend_taken": PAIRS,
    "pooled": B_TILES, "pool_done": B_TILES, "pool_taken": B_TILES,
    "mix_ready": KT, "x_in": 16 * ROWS, "y_taken": 2 * ROWS,
    "var_ready": 2, "rstd_ready": 1, "normed": 3, "scaled": 3, "pool_row": 3, "dve_row": 1,
    "out_landed": 16 * ROWS,
}
AHEAD = ("y_taken", "out_landed")


def trunk_kernel(nc, xt, xr, w, params, consts, pool_w, b_out, ln_gain, ln_bias, out):
    S_TABLE = schedule()
    with ExitStack() as ctx:
        def sb(name, shape, dt=F32):
            return ctx.enter_context(nc.sbuf_tensor(name, shape, dt))

        def bank(n):
            return ctx.enter_context(nc.psum_tensor(f"bank{n}", [P, 512], F32))

        sem = {name: ctx.enter_context(nc.semaphore(name)) for name in PER}
        raw_in = [ctx.enter_context(nc.semaphore(f"raw_in{i}")) for i in range(2)]
        first_x_in = [ctx.enter_context(nc.semaphore(f"first_x_in{j}")) for j in range(XP)]
        params_in = ctx.enter_context(nc.semaphore("params_in"))
        consts_in = ctx.enter_context(nc.semaphore("consts_in"))
        rest_in = ctx.enter_context(nc.semaphore("rest_in"))
        dve_ready = ctx.enter_context(nc.semaphore("dve_setup"))
        act_ready = ctx.enter_context(nc.semaphore("act_setup"))
        dve_step = ctx.enter_context(nc.semaphore("dve_step"))
        act_step = ctx.enter_context(nc.semaphore("act_step"))

        banks = [bank(n) for n in range(8)]

        raw = [sb(f"raw{i}", [P, 1024]) for i in range(2)]
        w_hi = [sb(f"w_hi{i}", [P, 1024], F32R) for i in range(3)]
        w_lo = [sb(f"w_lo{i}", [P, 1024], F32R) for i in range(3)]
        xt_hi = sb("xt_hi", [P, KT, TB], F32R)
        xt_lo = sb("xt_lo", [P, KT, TB], F32R)
        mix_hi = sb("mix_hi", [P, KT, TB], F32R)
        mix_lo = sb("mix_lo", [P, KT, TB], F32R)
        mixed = sb("mixed", [P, KT, TB])
        par = sb("par", [P, PR_N])
        nbin = sb("nbin", [P, IN_UNITS])
        kc = sb("kc", [P, K_N])
        pw = sb("pw", [P, B_TILES, P])
        bout = sb("bout", [P, D])
        gain = sb("gain", [P, D])
        beta = sb("beta", [P, D])
        lb = sb("lb", [P, A_HEADS])
        lb_tmp = sb("lb_tmp", [P, 3, A_HEADS])
        one_lb = sb("one_lb", [P, A_HEADS])
        nsink = sb("nsink", [P, 4])
        eps = sb("eps", [P, 1])
        ident = kc[:, K_ID:K_ID + P]
        mean_w = sb("mean_w", [P, P], F32R)
        masks = kc[:, K_MASK:K_N].bitcast(I32)
        lin = [sb(f"lin{i}", [P, TB]) for i in range(2)]
        sig = [sb(f"sig{i}", [P, TB]) for i in range(2)]
        q = sb("q", [P, TB])
        k = sb("k", [P, TB])
        logf = sb("logf", [P, TB])
        b16 = sb("b16", [P, TB])
        b128 = logf
        heads = [sb(f"heads{i}", [P, 10, TB]) for i in range(2)]
        N_K8, N_Q8, N_L, N_QIN, N_KEND, N_EIN, N_V = 0, 1, 2, 6, 7, 8, 9
        state = sb("state", [P, A_HEADS, P])
        kv_nat = [sb(f"kv_nat{i}", [P, 2 * P]) for i in range(2)]
        sct = [sb(f"sct{i}", [P, P]) for i in range(2)]
        osq = [sb(f"osq{i}", [P, TB]) for i in range(2)]
        kt_ = sb("kt_", [P, HD + TB])
        vt_ = sb("vt_", [P, HD + TB])
        qt = heads[1][:, 0:2, :].rearrange("p a t -> p (a t)")
        v_win = [heads[1][:, 2 + i, :] for i in range(2)]
        prob = [heads[1][:, 4 + i, :] for i in range(2)]
        pt = heads[1][:, 6, :]
        cmax = sb("cmax", [P, 2, 4])
        nm = sb("nm", [P, 2, 4])
        es = sb("es", [P, 2, 4])
        den = sb("den", [P, 2, 4])
        rden = sb("rden", [P, 2, 4])
        ub = sb("ub", [P, B_TILES, PAD + TB])
        spare = heads[1][:, 7:10, :].rearrange("p a t -> p (a t)")
        win = [spare[:, i * (PAD + TB):(i + 1) * (PAD + TB)] for i in range(2)]
        pooled = osq
        rows = heads[0][:, 0:8, :].rearrange("p (s h) t -> p s (h t)", s=ROWS)
        stats = sb("stats", [P, ROWS, 2, 6])
        mv = sb("mv", [P, ROWS, 2])
        rstd = sb("rstd", [P, ROWS])
        nmr = sb("nmr", [P, ROWS])

        def nth(b, name, n):
            return b * PER[name] + (n + (PER[name] if name in AHEAD else 0))

        def nth_before(b, name, n):
            return b * PER[name] + n

        def used_event(n):
            if n in U_GATE:
                return "mix_ready", U_GATE.index(n) + 1
            return "sig_used", 1 + [u for u in CHAINS if u not in U_GATE].index(n)

        def queries8(hb):
            return hb[:, N_Q8:N_Q8 + 2, :].rearrange("d a (c t) -> d (a c t)", t=P).rearrange("d (c t) -> d c t", t=2 * P)

        def logit_bank(p, j):
            return banks[(6, 2)[p % 2] + j]

        block = ctx.enter_context(nc.Block())

        @block.sync
        def _(sp):
            pieces = HEAD_PIECES + BODY_PIECES + BODY_PIECES[:AHEAD_LOADS]

            def load(b, i):
                kind, n = pieces[i]
                if i >= 2:
                    k2, n2 = pieces[i - 2]
                    if b is None:
                        sp.wait_ge(sem[f"{k2}_lo"], n2 + 1)
                    else:
                        if i - 2 >= len(HEAD_PIECES) + len(BODY_PIECES):
                            n2 += PER[f"{k2}_lo"]
                        sp.wait_ge(sem[f"{k2}_lo"], nth(b, f"{k2}_lo", n2 + 1))
                src = w[n % UNITS] if kind == "w" else xt[b + 1, n - XP]
                sp.dma_start(raw[i % 2][:], src).then_inc(raw_in[i % 2], 16)

            load(None, 0)
            for j in range(XP):
                sp.dma_start(mixed[:, 2 * j:2 * j + 2, :], xt[0, j].rearrange("p (a t) -> p a t", a=2)).then_inc(first_x_in[j], 16)
            load(None, 1)
            sp.dma_start(par[:], params).then_inc(params_in, 16)
            load(None, 2)
            sp.dma_start(kc[:], consts).then_inc(consts_in, 16)
            for i in range(3, len(HEAD_PIECES) + AHEAD_LOADS):
                load(None, i)
            with sp.Fori(0, BLOCKS) as b:
                for i in range(len(HEAD_PIECES) + AHEAD_LOADS, len(pieces)):
                    load(b, i)
                    if pieces[i] == ("w", 26):
                        sp.wait_ge(sem["chunk_done"], nth(b, "chunk_done", 12))
                        sp.wait_ge(sem["out_landed"], nth_before(b, "out_landed", 16 * ROWS))
                    if pieces[i] in (("w", 26), ("w", 27)):
                        for s in range(2 * pieces[i][1] - 52, 2 * pieces[i][1] - 50):
                            sp.dma_start(rows[:, s, :], xr[b, s]).then_inc(sem["x_in"], 16)
                for s in range(3):
                    sp.wait_ge(sem["pool_row"], nth(b, "pool_row", s + 1))
                    sp.dma_start(out[b, s], rows[:, s, :]).then_inc(sem["out_landed"], 16)
                sp.wait_ge(sem["dve_row"], nth(b, "dve_row", 1))
                sp.dma_start(out[b, 3], rows[:, 3, :]).then_inc(sem["out_landed"], 16)
            sp.wait_ge(sem["out_landed"], PER["out_landed"] * (BLOCKS + 1))
            total = len(HEAD_PIECES) + AHEAD_LOADS + BLOCKS * len(BODY_PIECES)
            for i in range(2):
                sp.wait_ge(raw_in[i], 16 * ((total + 1 - i) // 2))

        @block.gpsimd
        def _(pool):
            pool.sem_inc(sem["out_landed"], PER["out_landed"])
            pool.wait_ge(rest_in, 16 * 7)
            with pool.Fori(0, BLOCKS) as b:
                for s in range(3):
                    pool.wait_ge(sem["scaled"], nth(b, "scaled", s + 1))
                    nc.gpsimd.tensor_tensor(rows[:, s, :], rows[:, s, :], beta[:], ALU.add).then_inc(sem["pool_row"], 1)

        @block.tensor
        def _(pe):
            def project(b, n, mid):
                o = banks[unit_bank(n)]
                ws = w_slot(n)
                pe.wait_ge(sem["w_lo"], nth(b, "w_lo", n + 1))
                if n < 4:
                    pe.wait_ge(sem["y_taken"], nth_before(b, "y_taken", n + 1))
                else:
                    pe.wait_ge(sem["proj_taken"], nth(b, "proj_taken", n - 3 if n < 6 else n - 1))
                for kt in range(KT):
                    if n == 0 and kt % 2 == 0:
                        pe.wait_ge(sem["x_lo"], nth(b, "x_lo", kt // 2 + 1))
                    if kt == KT // 2:
                        mid()
                    if kt == KT - 1 and n == U_LOGITS:
                        pe.wait_ge(sem["proj_taken"], nth(b, "proj_taken", U_CK + 1))
                        pe.wait_ge(sem["y_taken"], nth_before(b, "y_taken", 2 * ROWS))
                        pe.wait_ge(dve_ready, 2)
                        pe.wait_ge(consts_in, 16)
                    if kt == KT - 1 and n == U_LOGITS + 1:
                        pe.wait_ge(sem["proj_taken"], nth(b, "proj_taken", U_CV + 1))
                    if kt == KT - 1 and n in (U_LOGITS + 2, U_LOGITS + 3):
                        pe.wait_ge(sem["p_exp"], nth(b, "p_exp", n - U_LOGITS - 1))
                    c = slice(kt * P, kt * P + P)
                    for step, (wx, xx) in enumerate(((w_hi, xt_hi), (w_hi, xt_lo), (w_lo, xt_hi))):
                        mm = nc.tensor.matmul(o[:], wx[ws][:, c], xx[:, kt, :],
                                              start=(kt == 0 and step == 0), stop=(kt == KT - 1 and step == 2))
                mm.then_inc(sem["unit_done"], 1)

            def project_out(b, n, mid):
                half, kp = divmod(n - IN_UNITS, 4)
                ws = w_slot(n)
                pe.wait_ge(sem["w_lo"], nth(b, "w_lo", n + 1))
                pe.wait_ge(sem["mix_ready"], nth(b, "mix_ready", 2 * kp + 2))
                if half == 1 and kp == 0:
                    pe.wait_ge(sem["o_taken"], nth(b, "o_taken", 16))
                    pe.wait_ge(sem["state_ready"], nth(b, "state_ready", 16))
                    pe.wait_ge(sem["mean_taken"], nth(b, "mean_taken", A_HEADS))
                    pe.wait_ge(sem["pool_taken"], nth(b, "pool_taken", B_TILES))
                for j in range(2):
                    if j == 1:
                        mid()
                    for s in range(ROWS):
                        if n == IN_UNITS and j == 0:
                            if s < 2:
                                pe.wait_ge(sem["proj_taken"], nth(b, "proj_taken", IN_UNITS - 1 + s))
                            elif s == 2:
                                pe.wait_ge(sem["scores_taken"], nth(b, "scores_taken", 16))
                            else:
                                pe.wait_ge(sem["turn_taken"], nth(b, "turn_taken", 16))
                        for step, (mx, wx) in enumerate(((mix_hi, w_hi), (mix_hi, w_lo), (mix_lo, w_hi))):
                            mm = nc.tensor.matmul(banks[4 * half + s][:], mx[:, 2 * kp + j, s * P:s * P + P],
                                                  wx[ws][:, j * 512:j * 512 + 512],
                                                  start=(kp == 0 and j == 0 and step == 0),
                                                  stop=(kp == 3 and j == 1 and step == 2))
                mm.then_inc(sem["unit_done"], 1)

            def v_turn(b, e):
                if e == 0:
                    pe.wait_ge(sem["proj_taken"], nth(b, "proj_taken", U_CV + 1))
                for p in range(PAIRS):
                    mm = nc.tensor.transpose(banks[4 + e][:, p * P:p * P + P], vt_[:, p * P + e * HD:p * P + e * HD + P], ident)
                mm.then_inc(sem["v_turned"], 1)

            def logits(b, p):
                for j in range(KV):
                    r = slice(j * HD, j * HD + HD)
                    for e in range(2):
                        at = p * P + e * HD
                        mm = nc.tensor.matmul(logit_bank(p, j)[:, e * P:e * P + P], qt[r, 2 * at:2 * at + P],
                                              kt_[r, at:at + P], start=True, stop=True)
                mm.then_inc(sem["logits_done"], 1)

            def p_turn(b, p):
                pe.wait_ge(sem["p_ready"], nth(b, "p_ready", p + 1))
                if p:
                    pe.wait_ge(sem["pt_taken"], nth(b, "pt_taken", p))
                else:
                    pe.wait_ge(sem["v_taken"], nth(b, "v_taken", 1))
                for h in range(4):
                    mm = nc.tensor.transpose(banks[4][:, h * P:h * P + P], prob[p % 2][:, h * P:h * P + P], ident)
                mm.then_inc(sem["p_turned"], 1)

            def attend(b, p):
                pe.wait_ge(sem["pt_taken"], nth(b, "pt_taken", p + 1))
                if p == 0:
                    pe.wait_ge(sem["v_taken"], nth(b, "v_taken", 2))
                else:
                    pe.wait_ge(sem["attend_taken"], nth(b, "attend_taken", p))
                pv = pt.rearrange("k (j e g t) -> k j e g t", j=2, e=2, g=2)
                ov = banks[5][:, 0:2 * P].rearrange("d (g e t) -> d g e t", g=2, e=2)
                for j in range(KV):
                    r = slice(j * HD, j * HD + HD)
                    for e in range(2):
                        mm = nc.tensor.matmul(ov[r, :, e, :], v_win[e][:, p * P + j * HD:p * P + j * HD + HD],
                                              pv[:, j, e, :, :], start=True, stop=True)
                mm.then_inc(sem["attend_done"], 1)

            def pool_mix(b, t):
                pe.wait_ge(rest_in, 16 * 7)
                pe.wait_ge(sem["pooled"], nth(b, "pooled", t + 1))
                if t == 0:
                    pe.wait_ge(sem["p_exp"], nth(b, "p_exp", PAIRS))
                else:
                    pe.wait_ge(sem["pool_taken"], nth(b, "pool_taken", t))
                nc.tensor.matmul(banks[7][:], pw[:, t, :], pooled[t][:], start=True, stop=True).then_inc(sem["pool_done"], 1)

            def chunk_scores(b, h, c):
                i = h * CHUNKS + c
                hb = heads[h % 2]
                t = slice(c * CHUNK, c * CHUNK + CHUNK)
                if c == 0:
                    pe.wait_ge(sem["prep_done"], nth(b, "prep_done", h + 1))
                    pe.wait_ge(sem["proj_taken"], nth(b, "proj_taken", U_HEAD[h] + 3))
                if i == 0:
                    pe.wait_ge(sem["p_exp"], nth(b, "p_exp", PAIRS))
                else:
                    pe.wait_ge(sem["turn_taken"], nth(b, "turn_taken", i))
                nc.tensor.transpose(banks[3][:, 0:P], hb[:, N_KEND, t], ident)
                nc.tensor.transpose(banks[3][:, P:2 * P], hb[:, N_V, t], ident).then_inc(sem["turned"], 1)
                if i:
                    pe.wait_ge(sem["scores_taken"], nth(b, "scores_taken", i))
                nc.tensor.matmul(banks[2][:, 0:P + 64], hb[:, N_K8, t], queries8(hb)[:, c, 0:P + 64], start=True, stop=True)
                for n, lv in list(enumerate(LEVELS))[1:]:
                    upper = hb[:, N_L + n, t].rearrange("d (g two t) -> d g two t", two=2, t=lv)[:, :, 1, :]
                    mm = nc.tensor.matmul(banks[2][:, P + 64 * n:P + 64 * n + 64], hb[:, N_L + n, t], upper, start=True, stop=True)
                mm.then_inc(sem["scores_done"], 1)

            def chunk_out(b, h, c):
                i = h * CHUNKS + c
                hb = heads[h % 2]
                t = slice(c * CHUNK, c * CHUNK + CHUNK)
                pe.wait_ge(sem["turn_taken"], nth(b, "turn_taken", i + 1))
                pe.wait_ge(sem["scores_taken"], nth(b, "scores_taken", i + 1))
                if i == 0:
                    pe.wait_ge(sem["attend_taken"], nth(b, "attend_taken", PAIRS))
                else:
                    pe.wait_ge(sem["state_ready"], nth(b, "state_ready", i))
                    pe.wait_ge(sem["o_taken"], nth(b, "o_taken", i))
                kn, vn = kv_nat[i % 2][:, 0:P], kv_nat[i % 2][:, P:2 * P]
                nc.tensor.matmul(banks[5][:, 0:P], kn, vn, start=True, stop=True)
                nc.tensor.matmul(banks[4][:, 0:P], vn, sct[i % 2][:], start=True, stop=False)
                nc.tensor.matmul(banks[4][:, 0:P], state[:, h, :], hb[:, N_QIN, t], start=False, stop=True).then_inc(sem["chunk_done"], 1)

            def norm(b, h):
                pe.wait_ge(act_ready, 2)
                pe.wait_ge(sem["squares_split"], nth(b, "squares_split", h + 1))
                if h:
                    pe.wait_ge(sem["mean_taken"], nth(b, "mean_taken", h))
                nc.tensor.matmul(banks[6][:], mean_w[:], mix_hi[:, M_A + h, :], start=True, stop=False)
                nc.tensor.matmul(banks[6][:], mean_w[:], mix_lo[:, M_A + h, :], start=False, stop=True).then_inc(sem["mean_done"], 1)

            steps = {"v_turn": v_turn, "logits": logits, "p_turn": p_turn, "attend": attend, "pool_mix": pool_mix,
                     "chunk_scores": chunk_scores, "chunk_out": chunk_out, "norm": norm}

            def run(b, todo):
                for name, *at in todo:
                    if name in steps:
                        steps[name](b, *at)

            with pe.Fori(0, BLOCKS) as b:
                for n in range(UNITS):
                    (project if n < IN_UNITS else project_out)(b, n, lambda: run(b, S_TABLE[n][0]))
                    run(b, S_TABLE[n][1])
            pe.wait_ge(sem["y_taken"], PER["y_taken"] * (BLOCKS + 1))
            pe.sem_inc(sem["unit_done"], 2)

        @block.scalar
        def _(act):
            own = [0]

            def counted():
                own[0] += 1
                return 1

            act.preload_act_table_set("natural_log_exp_and_others")

            def high_x(j, src):
                j %= XP
                nc.scalar.activation(xt_hi[:, 2 * j:2 * j + 2, :], src, ACT.Copy).then_inc(sem["x_hi"], 1)

            def high_w(u, src):
                nc.scalar.activation(w_hi[w_slot(u)][:], src[:], ACT.Copy).then_inc(sem["w_hi"], 1)

            landed_count = [0, 0]

            def split_high(b, i, kind, n):
                landed_count[i % 2] += 1
                if b is None:
                    act.wait_ge(raw_in[i % 2], 16 * landed_count[i % 2])
                else:
                    act.wait_ge(raw_in[i % 2], b * (8 * len(BODY_PIECES)) + 16 * landed_count[i % 2])
                if kind == "x":
                    high_x(n, raw[i % 2][:].rearrange("p (a t) -> p a t", a=2))
                else:
                    high_w(n, raw[i % 2])

            split_high(None, 0, *HEAD_PIECES[0])
            for j in range(XP):
                act.wait_ge(first_x_in[j], 16)
                high_x(j, mixed[:, 2 * j:2 * j + 2, :])
            for i in (1, 2):
                split_high(None, i, *HEAD_PIECES[i])
            act.wait_ge(dve_ready, 1)
            for g in range(4):
                r = slice((g % 2) * HD, (g % 2) * HD + HD)
                act.dma_start(pw[r, g // 2, r], pool_w[g]).then_inc(rest_in, 16)
            for dst, src in ((bout, b_out), (gain, ln_gain), (beta, ln_bias)):
                act.dma_start(dst[:], src.partition_broadcast(P)).then_inc(rest_in, 16)
            nc.scalar.activation(lb_tmp[:, 1, :], lb_tmp[:, 0, :], ACT.Exp).then_inc(act_ready, 1)
            act.wait_ge(consts_in, 16)
            nc.scalar.activation(mean_w[:], kc[:, K_MEAN:K_MEAN + P], ACT.Copy).then_inc(act_ready, 1)
            act.wait_ge(dve_ready, 2)
            act.wait_ge(params_in, 16)
            for i in (3, 4):
                act.wait_ge(sem["unit_done"], i - 2)
                split_high(None, i, *HEAD_PIECES[i])

            def bias(n):
                return par[:, PR_BIN + n:PR_BIN + n + 1]

            def take_unit(b, n):
                src = banks[unit_bank(n)][:]
                if n in CHAINS:
                    c = CHAINS.index(n)
                    if c >= 2:
                        name, count = used_event(CHAINS[c - 2])
                        act.wait_ge(sem[name], nth(b, name, count))
                    if n not in U_HEAD:
                        nc.scalar.activation(lin[c % 2][:], src, ACT.Identity, bias=bias(n))
                    nc.scalar.activation(sig[c % 2][:], src, ACT.Exp, bias=nbin[:, n:n + 1], scale=-1.0).then_inc(sem["proj_taken"], 1)
                    return
                if n < U_CK:
                    dst = qt.rearrange("p (c g t) -> p c g t", g=2, t=HD)[:, :, n - U_CQ, :]
                    src = src.rearrange("p (c t) -> p c t", t=HD)
                elif n == U_CK:
                    dst = kt_[:, HD:HD + TB]
                elif n == U_CV:
                    dst = vt_[:, HD:HD + TB]
                elif n in U_B:
                    dst = ub[:, U_B.index(n), PAD:PAD + TB]
                else:
                    h = U_HEAD.index(n - 2)
                    dst = heads[h % 2][:, N_V, :]
                    if h == 1:
                        act.wait_ge(sem["attend_done"], nth(b, "attend_done", PAIRS))
                    elif h >= 2:
                        act.wait_ge(sem["chunk_done"], nth(b, "chunk_done", 4 * (h - 1)))
                nc.scalar.activation(dst, src, ACT.Identity, bias=bias(n)).then_inc(sem["proj_taken"], 1)

            def sigmoid(b, c):
                act.wait_ge(sem["d_ready"], nth(b, "d_ready", c + 1))
                nc.scalar.activation(sig[c % 2][:], sig[c % 2][:], ACT.Ln).then_inc(act_step, counted())
                act.wait_ge(act_step, own[0])
                nc.scalar.activation(sig[c % 2][:], sig[c % 2][:], ACT.Exp, scale=-1.0).then_inc(sem["sig_ready"], 1)

            def v_turn(b, e):
                act.wait_ge(sem["v_turned"], nth(b, "v_turned", e + 1))
                nc.scalar.activation(v_win[e], banks[4 + e][:], ACT.Copy).then_inc(sem["v_taken"], 1)

            def logits(b, p):
                act.wait_ge(sem["max_ready"], nth(b, "max_ready", p + 1))
                for h in range(4):
                    j, e = divmod(h, 2)
                    nc.scalar.activation(prob[p % 2][:, h * P:h * P + P], logit_bank(p, j)[:, e * P:e * P + P], ACT.Exp,
                                         bias=nm[:, p % 2, h:h + 1], scale=SCALE, accum_out=den[:, p % 2, h:h + 1])
                ins = nc.scalar.activation(es[:, p % 2, :], es[:, p % 2, :], ACT.Exp)
                ins.then_inc(sem["p_exp"], 1)

            def p_turn(b, p):
                act.wait_ge(sem["p_turned"], nth(b, "p_turned", p + 1))
                if p:
                    act.wait_ge(sem["attend_done"], nth(b, "attend_done", p))
                nc.scalar.activation(pt, banks[4][:], ACT.Copy).then_inc(sem["pt_taken"], 1)

            def attend(b, p):
                act.wait_ge(sem["attend_done"], nth(b, "attend_done", p + 1))
                nc.scalar.activation(mixed[:, M_C:M_C + 2, p * P:p * P + P], banks[5][:, 0:2 * P].rearrange("d (g t) -> d g t", g=2),
                                     ACT.Copy).then_inc(sem["attend_taken"], 1)
                if p == PAIRS - 1:
                    for buf in (kt_, vt_):
                        nc.scalar.activation(buf[:, 0:HD], buf[:, TB:TB + HD], ACT.Copy)

            def pool_mix(b, t):
                act.wait_ge(sem["pool_done"], nth(b, "pool_done", t + 1))
                nc.scalar.activation(mixed[:, M_B + t, :], banks[7][:], ACT.Copy,
                                     scale=par[:, PR_PSC + t:PR_PSC + t + 1]).then_inc(sem["pool_taken"], 1)

            def log_decay(b, h):
                act.wait_ge(sem["floored"], nth(b, "floored", h + 1))
                nc.scalar.activation(logf[:], logf[:], ACT.Ln).then_inc(sem["logf_ready"], 1)

            def exponentials(b, h, part):
                hb = heads[h % 2]
                base = 6 * h
                if part == 0:
                    act.wait_ge(sem["diff_ready"], nth(b, "diff_ready", base + 1))
                    nc.scalar.activation(queries8(hb)[:, :, 0:P], hb[:, N_K8, :].rearrange("d (c t) -> d c t", t=P), ACT.Exp)
                    nc.scalar.activation(hb[:, N_EIN, :], b128[:], ACT.Exp)
                    nc.scalar.activation(hb[:, N_K8, :], hb[:, N_K8, :], ACT.Exp, scale=-1.0).then_inc(sem["exp_ready"], 1)
                    act.wait_ge(sem["diff_ready"], nth(b, "diff_ready", base + 2))
                    level8 = queries8(hb)[:, :, P:P + 64]
                    nc.scalar.activation(level8, level8, ACT.Exp).then_inc(sem["exp_ready"], 1)
                for n in () if part == 0 else (1, 2, 3):
                    lv = LEVELS[n]
                    act.wait_ge(sem["diff_ready"], nth(b, "diff_ready", base + 2 + n))
                    v = hb[:, N_L + n, :].rearrange("d (g two t) -> d g two t", two=2, t=lv)
                    up = b16[:].rearrange("d (g two t) -> d g two t", two=2, t=lv) if lv == 16 else v
                    nc.scalar.activation(v[:, :, 0, :], v[:, :, 0, :], ACT.Exp, scale=-1.0)
                    nc.scalar.activation(v[:, :, 1, :], up[:, :, 1, :], ACT.Exp).then_inc(sem["exp_ready"], 1)
                if part == 1:
                    act.wait_ge(sem["diff_ready"], nth(b, "diff_ready", base + 6))
                    nc.scalar.activation(hb[:, N_KEND, :], hb[:, N_KEND, :], ACT.Exp, scale=-1.0).then_inc(sem["exp_ready"], 1)

            def chunk_scores(b, h, c):
                i = h * CHUNKS + c
                act.wait_ge(sem["turned"], nth(b, "turned", i + 1))
                if i >= 2:
                    act.wait_ge(sem["chunk_done"], nth(b, "chunk_done", i - 1))
                nc.scalar.activation(kv_nat[i % 2][:], banks[3][:, 0:2 * P], ACT.Copy).then_inc(sem["turn_taken"], 1)

            def chunk_out(b, h, c):
                i = h * CHUNKS + c
                t = slice(c * CHUNK, c * CHUNK + CHUNK)
                act.wait_ge(sem["chunk_done"], nth(b, "chunk_done", i + 1))
                if h >= 2 and c == 0:
                    act.wait_ge(sem["mean_done"], nth(b, "mean_done", h - 1))
                    act.wait_ge(sem["norm_done"], nth(b, "norm_done", h - 1))
                nc.scalar.activation(mixed[:, M_A + h, t], banks[4][:, 0:P], ACT.Copy)
                nc.scalar.activation(osq[h % 2][:, t], banks[4][:, 0:P], ACT.Square)
                nc.scalar.activation(mix_hi[:, M_A + h, t], banks[4][:, 0:P], ACT.Square).then_inc(sem["o_taken"], 1)

            def norm(b, h):
                act.wait_ge(sem["mean_done"], nth(b, "mean_done", h + 1))
                nc.scalar.activation(osq[h % 2][:], banks[6][:], ACT.Ln, bias=eps[:]).then_inc(sem["mean_taken"], 1)
                act.wait_ge(sem["mean_taken"], nth(b, "mean_taken", h + 1))
                nc.scalar.activation(osq[h % 2][:], osq[h % 2][:], ACT.Exp, scale=-0.5).then_inc(sem["inv_ready"], 1)

            steps = {"v_turn": v_turn, "logits": logits, "p_turn": p_turn, "attend": attend, "pool_mix": pool_mix, "sigmoid": sigmoid,
                     "log_decay": log_decay, "exponentials": exponentials, "chunk_scores": chunk_scores, "chunk_out": chunk_out, "norm": norm}

            def run(b, todo):
                for name, *at in todo:
                    if name in steps:
                        steps[name](b, *at)

            with act.Fori(0, BLOCKS) as b:
                i = len(HEAD_PIECES)
                for n in range(UNITS):
                    run(b, S_TABLE[n][0])
                    act.wait_ge(sem["unit_done"], nth(b, "unit_done", n + 1))
                    if n < IN_UNITS:
                        take_unit(b, n)
                    for piece in SPLITS[n]:
                        split_high(b, i, *piece)
                        i += 1
                    run(b, S_TABLE[n][1])
                split_high(b, i, *IN_NEXT[0])
                split_high(b, i + 1, *IN_NEXT[1])
                for half in range(2):
                    two = slice(2 * half, 2 * half + 2)
                    act.wait_ge(sem["var_ready"], nth(b, "var_ready", half + 1))
                    nc.scalar.activation(rstd[:, two], mv[:, two, 1], ACT.Ln, bias=eps[:]).then_inc(act_step, counted())
                    act.wait_ge(act_step, own[0])
                    ins = nc.scalar.activation(rstd[:, two], rstd[:, two], ACT.Exp, scale=-0.5)
                    if half == 0:
                        ins.then_inc(act_step, counted())
                        act.wait_ge(act_step, own[0])
                    else:
                        ins.then_inc(sem["rstd_ready"], 1)
                        act.wait_ge(sem["rstd_ready"], nth(b, "rstd_ready", 1))
                    normalised = ((0, 1), (2,))[half]
                    for s in normalised:
                        nc.scalar.activation(nmr[:, s:s + 1], nmr[:, s:s + 1], ACT.Copy, scale=rstd[:, s:s + 1]).then_inc(act_step, counted())
                    act.wait_ge(act_step, own[0])
                    for s in normalised:
                        nc.scalar.activation(rows[:, s, :], rows[:, s, :], ACT.Identity, bias=nmr[:, s:s + 1],
                                             scale=rstd[:, s:s + 1]).then_inc(sem["normed"], 1)
                        if s:
                            act.wait_ge(sem["unit_done"], nth(b + 1, "unit_done", s))
                            split_high(b, i + s + 1, *IN_NEXT[s + 1])
                act.sem_clear(act_step)
                own[0] = 0

        @block.vector
        def _(dve):
            own = [0]

            def counted():
                own[0] += 1
                return 1

            dve.sem_inc(sem["y_taken"], PER["y_taken"])
            for buf in (pw, state, sct[0], sct[1], kt_, vt_, ub):
                nc.vector.memset(buf[:], 0.0).then_inc(dve_step, counted())
            nc.vector.memset(eps[:], EPS).then_inc(dve_step, counted())

            def split_low(b, i, kind, n):
                if b is None:
                    dve.wait_ge(sem[f"{kind}_hi"], n + 1)
                else:
                    dve.wait_ge(sem[f"{kind}_hi"], nth(b, f"{kind}_hi", n + 1))
                if kind == "w":
                    nc.vector.tensor_tensor(w_lo[w_slot(n)][:], raw[i % 2][:], w_hi[w_slot(n)][:].bitcast(F32), ALU.subtract).then_inc(sem["w_lo"], 1)
                else:
                    low_x(n % XP, raw[i % 2][:].rearrange("p (a t) -> p a t", a=2))

            def low_x(j, src):
                pair = slice(2 * j, 2 * j + 2)
                nc.vector.tensor_tensor(xt_lo[:, pair, :], src, xt_hi[:, pair, :].bitcast(F32), ALU.subtract).then_inc(sem["x_lo"], 1)

            split_low(None, 0, *HEAD_PIECES[0])
            for j in range(XP):
                dve.wait_ge(sem["x_hi"], j + 1)
                low_x(j, mixed[:, 2 * j:2 * j + 2, :])
            split_low(None, 1, *HEAD_PIECES[1])
            dve.wait_ge(params_in, 16)
            dve.wait_ge(dve_step, own[0])
            logit = par[:, PR_LB:PR_LB + A_HEADS]
            nc.vector.tensor_tensor(lb_tmp[:, 0, :], logit, logit, ALU.subtract).then_inc(dve_ready, 1)
            split_low(None, 2, *HEAD_PIECES[2])
            nc.vector.tensor_scalar(nbin[:], par[:, PR_BIN:PR_BIN + IN_UNITS], -1.0, None, ALU.mult).then_inc(dve_step, counted())
            nc.vector.tensor_scalar(nsink[:], par[:, PR_SINK:PR_SINK + 4], -1.0, None, ALU.mult).then_inc(dve_step, counted())
            dve.wait_ge(act_ready, 1)
            nc.vector.reciprocal(lb_tmp[:, 2, :], lb_tmp[:, 1, :]).then_inc(dve_step, counted())
            dve.wait_ge(dve_step, own[0])
            nc.vector.tensor_tensor(lb_tmp[:, 2, :], lb_tmp[:, 1, :], lb_tmp[:, 2, :], ALU.mult).then_inc(dve_step, counted())
            dve.wait_ge(dve_step, own[0])
            nc.vector.tensor_tensor(lb[:], lb_tmp[:, 2, :], lb_tmp[:, 2, :], ALU.subtract).then_inc(dve_step, counted())
            dve.wait_ge(dve_step, own[0])
            nc.vector.tensor_scalar(lb[:], lb[:], 0.0, None, ALU.max).then_inc(dve_step, counted())
            dve.wait_ge(dve_step, own[0])
            nc.vector.tensor_scalar(one_lb[:], lb[:], -1.0, 1.0, ALU.mult, ALU.add).then_inc(dve_ready, 1)
            dve.wait_ge(dve_ready, 2)
            for i in (3, 4):
                split_low(None, i, *HEAD_PIECES[i])
            dve.sem_clear(dve_step)
            own[0] = 0

            def start_sigmoid(b, c):
                dve.wait_ge(sem["proj_taken"], nth(b, "proj_taken", CHAINS[c] + 1))
                nc.vector.tensor_scalar(sig[c % 2][:], sig[c % 2][:], EXP_CAP, 1.0, ALU.min, ALU.add).then_inc(sem["d_ready"], 1)

            def use_sigmoid(b, c):
                n = CHAINS[c]
                dve.wait_ge(sem["sig_ready"], nth(b, "sig_ready", c + 1))
                s, x = sig[c % 2][:], lin[c % 2][:]
                if n in U_GATE:
                    m = U_GATE.index(n)
                    if m < M_B:
                        dve.wait_ge(sem["attend_taken"], nth(b, "attend_taken", PAIRS))
                    elif m < M_A:
                        dve.wait_ge(sem["pool_taken"], nth(b, "pool_taken", B_TILES))
                    nc.vector.tensor_tensor(s, s, x, ALU.mult).then_inc(dve_step, counted())
                    dve.wait_ge(dve_step, own[0])
                    nc.vector.tensor_tensor(s, s, mixed[:, m, :], ALU.mult).then_inc(dve_step, counted())
                    dve.wait_ge(dve_step, own[0])
                    nc.vector.tensor_copy(mix_hi[:, m, :], s).then_inc(dve_step, counted())
                    dve.wait_ge(dve_step, own[0])
                    nc.vector.tensor_tensor(mix_lo[:, m, :], s, mix_hi[:, m, :].bitcast(F32), ALU.subtract).then_inc(sem["mix_ready"], 1)
                    return
                if n in U_HEAD:
                    h = U_HEAD.index(n)
                    nc.vector.tensor_scalar(s, s, one_lb[:, h:h + 1], lb[:, h:h + 1], ALU.mult, ALU.add).then_inc(dve_step, counted())
                    dve.wait_ge(dve_step, own[0])
                    nc.vector.tensor_scalar(logf[:], s, F_FLOOR, None, ALU.max).then_inc(sem["floored"], 1)
                    nc.vector.tensor_scalar(k[:], s, -1.0, 1.0, ALU.mult, ALU.add).then_inc(sem["sig_used"], 1)
                else:
                    nc.vector.tensor_tensor(q[:], x, s, ALU.mult).then_inc(sem["sig_used"], 1)

            def windows(b, t):
                dve.wait_ge(sem["proj_taken"], nth(b, "proj_taken", U_B[t] + 1))
                n = PAD + TB
                a, c = win
                u = ub[:, t, :]
                nc.vector.tensor_tensor(a[:, 1:n], u[:, 1:n], u[:, 0:n - 1], ALU.add).then_inc(dve_step, counted())
                dve.wait_ge(dve_step, own[0])
                if t == 1:
                    nc.vector.tensor_tensor(c[:, 3:n], a[:, 3:n], a[:, 1:n - 2], ALU.add).then_inc(dve_step, counted())
                    dve.wait_ge(dve_step, own[0])
                    nc.vector.tensor_tensor(a[:, 7:n], c[:, 7:n], c[:, 3:n - 4], ALU.add).then_inc(dve_step, counted())
                    dve.wait_ge(dve_step, own[0])
                half = POOL_WINDOWS[2 * t]
                nc.vector.scalar_tensor_tensor(out=c[:, PAD:n], in0=a[:, PAD - half:n - half], scalar=kc[:, K_UP:K_UP + 1],
                                               in1=a[:, PAD:n], op0=ALU.mult, op1=ALU.add).then_inc(dve_step, counted())
                dve.wait_ge(dve_step, own[0])
                nc.vector.tensor_tensor(c[:, PAD:2 * PAD], c[:, PAD:2 * PAD],
                                        kc[:, K_CORR + t * PAD:K_CORR + (t + 1) * PAD], ALU.mult).then_inc(dve_step, counted())
                dve.wait_ge(dve_step, own[0])
                nc.vector.scalar_tensor_tensor(out=pooled[t][:], in0=c[:, PAD:n], scalar=kc[:, K_WINV + t:K_WINV + t + 1],
                                               in1=u[:, PAD:n], op0=ALU.mult, op1=ALU.subtract).then_inc(sem["pooled"], 1)
                dve.wait_ge(sem["pooled"], nth(b, "pooled", t + 1))
                nc.vector.tensor_copy(ub[:, t, 0:PAD], ub[:, t, TB:TB + PAD])
                nc.vector.memset(kc[:, K_CORR + t * PAD:K_CORR + (t + 1) * PAD], 1.0)

            def logits(b, p):
                dve.wait_ge(sem["logits_done"], nth(b, "logits_done", p + 1))
                if p == 0:
                    dve.wait_ge(consts_in, 16)
                    for j in range(KV):
                        v = logit_bank(p, j)[:, 0:P]
                        nc.vector.tensor_tensor(v, v, kc[:, K_PEN:K_PEN + P], ALU.add).then_inc(dve_step, counted())
                    dve.wait_ge(dve_step, own[0])
                    nc.vector.memset(kc[:, K_PEN:K_PEN + P], 0.0).then_inc(dve_step, counted())
                for j in range(KV):
                    nc.vector.tensor_reduce(cmax[:, p % 2, 2 * j:2 * j + 2],
                                                 logit_bank(p, j)[:, 0:2 * P].rearrange("q (e s) -> q e s", e=2), AX.X, ALU.max).then_inc(dve_step, counted())
                dve.wait_ge(dve_step, own[0])
                nc.vector.scalar_tensor_tensor(out=nm[:, p % 2, :], in0=cmax[:, p % 2, :], scalar=-SCALE, in1=nsink[:],
                                                    op0=ALU.mult, op1=ALU.min).then_inc(dve_step, counted())
                dve.wait_ge(dve_step, own[0])
                nc.vector.tensor_tensor(es[:, p % 2, :], nm[:, p % 2, :], nsink[:], ALU.subtract).then_inc(sem["max_ready"], 1)

            def normalise(b, p):
                dve.wait_ge(sem["p_exp"], nth(b, "p_exp", p + 1))
                nc.vector.tensor_tensor(den[:, p % 2, :], den[:, p % 2, :], es[:, p % 2, :], ALU.add).then_inc(dve_step, counted())
                dve.wait_ge(dve_step, own[0])
                nc.vector.reciprocal(rden[:, p % 2, :], den[:, p % 2, :]).then_inc(dve_step, counted())
                dve.wait_ge(dve_step, own[0])
                v = prob[p % 2].rearrange("q (h s) -> q h s", h=4)
                nc.vector.tensor_tensor(v, v, rden[:, p % 2, :].unsqueeze(2).broadcast_to([P, 4, P]), ALU.mult).then_inc(sem["p_ready"], 1)

            def differences(b, h):
                hb = heads[h % 2]
                dve.wait_ge(sem["logf_ready"], nth(b, "logf_ready", h + 1))
                if h == 0:
                    dve.wait_ge(sem["out_landed"], nth_before(b, "out_landed", 16 * ROWS))
                if h == 1:
                    dve.wait_ge(sem["attend_done"], nth(b, "attend_done", PAIRS))
                if h >= 2:
                    dve.wait_ge(sem["chunk_done"], nth(b, "chunk_done", 4 * (h - 1)))
                nc.vector.tensor_tensor_scan(b16[:], kc[:, K_R16:K_R16 + TB], logf[:], 0.0, ALU.mult, ALU.add).then_inc(dve_step, counted())
                dve.wait_ge(dve_step, own[0])
                nc.vector.tensor_tensor_scan(b128[:], kc[:, K_R128:K_R128 + TB], logf[:], 0.0, ALU.mult, ALU.add).then_inc(dve_step, counted())
                dve.wait_ge(dve_step, own[0])

                def minus(dst, src, seg, at, n=None):
                    n = n or seg
                    v = src[:].rearrange("d (g t) -> d g t", t=seg)
                    return nc.vector.tensor_tensor(dst.rearrange("d (g t) -> d g t", t=seg)[:, :, 0:n], v[:, :, 0:n],
                                                   v[:, :, at:at + 1].broadcast_to([P, TB // seg, n]), ALU.subtract)

                minus(hb[:, N_K8, :], b16, 8, 3).then_inc(sem["diff_ready"], 1)
                v = b16[:].rearrange("d (c g t) -> d c g t", g=P // 16, t=16)
                nc.vector.tensor_tensor(queries8(hb)[:, :, P:P + 64].rearrange("d c (g t) -> d c g t", t=8), v[:, :, :, 8:16],
                                        v[:, :, :, 3:4].broadcast_to([P, CHUNKS, P // 16, 8]), ALU.subtract).then_inc(sem["diff_ready"], 1)
                for n, lv in list(enumerate(LEVELS))[1:]:
                    minus(hb[:, N_L + n, :], b16 if lv <= 16 else b128, 2 * lv, lv - 1,
                          lv if lv == 16 else None).then_inc(sem["diff_ready"], 1)
                minus(hb[:, N_KEND, :], b128, CHUNK, CHUNK - 1).then_inc(sem["diff_ready"], 1)

            def products(b, h, part):
                hb = heads[h % 2]
                base = 6 * h
                if part == 0:
                    dve.wait_ge(sem["exp_ready"], nth(b, "exp_ready", base + 1))
                    v = queries8(hb)[:, :, 0:P]
                    nc.vector.tensor_tensor(v, v, q[:].rearrange("d (c t) -> d c t", t=P), ALU.mult).then_inc(dve_step, counted())
                    nc.vector.tensor_tensor(hb[:, N_K8, :], hb[:, N_K8, :], k[:], ALU.mult).then_inc(dve_step, counted())
                    nc.vector.tensor_tensor(hb[:, N_QIN, :], hb[:, N_EIN, :], q[:], ALU.mult).then_inc(dve_step, counted())
                    dve.wait_ge(sem["exp_ready"], nth(b, "exp_ready", base + 2))
                    v = queries8(hb)[:, :, P:P + 64].rearrange("d c (g t) -> d c g t", t=8)
                    nc.vector.tensor_tensor(v, v, q[:].rearrange("d (c g t) -> d c g t", g=P // 16, t=16)[:, :, :, 8:16],
                                            ALU.mult).then_inc(dve_step, counted())
                for n in (1,) if part == 0 else (2, 3):
                    lv = LEVELS[n]
                    dve.wait_ge(sem["exp_ready"], nth(b, "exp_ready", base + 2 + n))
                    for half, src in enumerate((k, q)):
                        v = hb[:, N_L + n, :].rearrange("d (g two t) -> d g two t", two=2, t=lv)[:, :, half, :]
                        sv = src[:].rearrange("d (g two t) -> d g two t", two=2, t=lv)[:, :, half, :]
                        nc.vector.tensor_tensor(v, v, sv, ALU.mult).then_inc(dve_step, counted())
                if part == 1:
                    dve.wait_ge(sem["exp_ready"], nth(b, "exp_ready", base + 6))
                    nc.vector.tensor_tensor(hb[:, N_KEND, :], hb[:, N_KEND, :], k[:], ALU.mult).then_inc(sem["prep_done"], 1)

            def chunk_scores(b, h, c):
                i = h * CHUNKS + c
                dve.wait_ge(sem["scores_done"], nth(b, "scores_done", i + 1))
                if i >= 2:
                    dve.wait_ge(sem["chunk_done"], nth(b, "chunk_done", i - 1))
                nc.vector.tensor_copy(sct[i % 2][0:64, 64:P], banks[2][0:64, P + 192:P + 256]).then_inc(dve_step, counted())
                dve.wait_ge(dve_step, own[0])
                nc.vector.copy_predicated(sct[i % 2][:], masks[:, 0:P], banks[2][:, 0:P]).then_inc(dve_step, counted())
                dve.wait_ge(dve_step, own[0])
                for n, lv in enumerate(LEVELS[:-1]):
                    cols = slice(P + 64 * n, P + 64 * n + 64)
                    dst = sct[i % 2][:].rearrange("s (g two t) -> s g two t", two=2, t=lv)[:, :, 1, :]
                    ins = nc.vector.copy_predicated(dst, masks[:, cols].rearrange("s (g t) -> s g t", t=lv),
                                                    banks[2][:, cols].rearrange("s (g t) -> s g t", t=lv))
                    if n < 2:
                        ins.then_inc(dve_step, counted())
                        dve.wait_ge(dve_step, own[0])
                ins.then_inc(sem["scores_taken"], 1)

            def chunk_out(b, h, c):
                i = h * CHUNKS + c
                dve.wait_ge(sem["chunk_done"], nth(b, "chunk_done", i + 1))
                last = c * CHUNK + CHUNK - 1
                nc.vector.scalar_tensor_tensor(out=state[:, h, :], in0=state[:, h, :], scalar=heads[h % 2][:, N_EIN, last:last + 1],
                                               in1=banks[5][:, 0:P], op0=ALU.mult, op1=ALU.add).then_inc(sem["state_ready"], 1)

            def split_squares(b, h):
                dve.wait_ge(sem["o_taken"], nth(b, "o_taken", h * CHUNKS + CHUNKS))
                nc.vector.tensor_tensor(mix_lo[:, M_A + h, :], osq[h % 2][:], mix_hi[:, M_A + h, :].bitcast(F32), ALU.subtract).then_inc(sem["squares_split"], 1)

            def norm(b, h):
                dve.wait_ge(sem["inv_ready"], nth(b, "inv_ready", h + 1))
                m = mixed[:, M_A + h, :]
                nc.vector.scalar_tensor_tensor(out=m, in0=m, scalar=par[:, PR_GAIN + h:PR_GAIN + h + 1], in1=osq[h % 2][:],
                                               op0=ALU.mult, op1=ALU.mult).then_inc(sem["norm_done"], 1)

            def residual(b, s):
                dve.wait_ge(rest_in, 16 * 7)
                dve.wait_ge(sem["x_in"], nth(b, "x_in", 16 * ROWS))
                nc.vector.scalar_tensor_tensor(out=rows[:, s, :], in0=rows[:, s, :], scalar=ALPHA, in1=bout[:],
                                                    op0=ALU.mult, op1=ALU.add).then_inc(dve_step, counted())

            def take_two(b, half, s0, split=None):
                cols = slice(512 * half, 512 * half + 512)
                for s in (s0, s0 + 1):
                    r = rows[:, s, cols]
                    nc.vector.tensor_tensor(r, banks[4 * half + s][:], r, ALU.add).then_inc(sem["y_taken"], 1)
                if split:
                    split_low(b, *split)
                for s in (s0, s0 + 1):
                    dve.wait_ge(sem["y_taken"], nth(b, "y_taken", 4 * half + s + 1))
                    nc.vector.bn_stats(stats[:, s, half, :], rows[:, s, cols]).then_inc(dve_step, counted())

            def take_rows(b, half):
                dve.wait_ge(sem["unit_done"], nth(b, "unit_done", IN_UNITS + 4))
                dve.wait_ge(dve_step, own[0])
                for s in (0, 2):
                    take_two(b, half, s)

            def moments(s0):
                two = slice(s0, s0 + 2)
                dve.wait_ge(dve_step, own[0])
                for s in (s0, s0 + 1):
                    nc.vector.bn_aggr(mv[:, s, :], stats[:, s, :, :].rearrange("p a c -> p (a c)")).then_inc(dve_step, counted())
                dve.wait_ge(dve_step, own[0])
                nc.vector.tensor_scalar(nmr[:, two], mv[:, two, 0], -1.0, None, ALU.mult).then_inc(sem["var_ready"], 1)

            def last_rows(b, i):
                dve.wait_ge(sem["unit_done"], nth(b, "unit_done", UNITS))
                take_two(b, 1, 0, (i, *IN_NEXT[0]))
                moments(0)
                take_two(b, 1, 2, (i + 1, *IN_NEXT[1]))
                moments(2)
                for s in range(3):
                    if s == 2:
                        split_low(b, i + 2, *IN_NEXT[2])
                    dve.wait_ge(sem["normed"], nth(b, "normed", s + 1))
                    nc.vector.tensor_tensor(rows[:, s, :], rows[:, s, :], gain[:], ALU.mult).then_inc(sem["scaled"], 1)
                dve.wait_ge(sem["var_ready"], nth(b, "var_ready", 2))
                nc.vector.scalar_tensor_tensor(out=rows[:, 3, :], in0=rows[:, 3, :], scalar=nmr[:, 3:4], in1=gain[:],
                                               op0=ALU.add, op1=ALU.mult).then_inc(dve_step, counted())
                split_low(b, i + 3, *IN_NEXT[3])
                dve.wait_ge(sem["rstd_ready"], nth(b, "rstd_ready", 1))
                dve.wait_ge(dve_step, own[0])
                nc.vector.scalar_tensor_tensor(out=rows[:, 3, :], in0=rows[:, 3, :], scalar=rstd[:, 3:4], in1=beta[:],
                                               op0=ALU.mult, op1=ALU.add).then_inc(sem["dve_row"], 1)

            steps = {"windows": windows, "logits": logits, "normalise": normalise, "differences": differences, "products": products,
                     "use_sigmoid": use_sigmoid, "chunk_scores": chunk_scores, "chunk_out": chunk_out, "norm": norm,
                     "split_squares": split_squares, "residual": residual, "take_rows": take_rows}

            def run(b, todo):
                for name, *at in todo:
                    if name in steps:
                        steps[name](b, *at)

            with dve.Fori(0, BLOCKS) as b:
                i = len(HEAD_PIECES)
                for n in range(UNITS):
                    run(b, S_TABLE[n][0])
                    if n in CHAINS:
                        start_sigmoid(b, CHAINS.index(n))
                    for piece in SPLITS[n]:
                        split_low(b, i, *piece)
                        i += 1
                    run(b, S_TABLE[n][1])
                last_rows(b, i)
                dve.sem_clear(dve_step)
                own[0] = 0


def kernel(x, w_in, b_in, lb_logits, a_norm_gain, pool_w, pool_scale, attn_sinks, w_out, b_out, ln_gain, ln_bias):
    import concourse.bacc as _bacc
    from concourse.bass_utils import run_bass_kernel_spmd as _run

    x, w_in, w_out = np.asarray(x)[0], np.asarray(w_in)[0], np.asarray(w_out)[0]
    xt = x.reshape(BLOCKS, TB, XP, 2, P).transpose(0, 2, 4, 3, 1).reshape(BLOCKS, XP, P, 2 * TB)
    xt = np.concatenate([xt, xt[:1]])
    xr = x.reshape(BLOCKS, ROWS, P, D)
    cols = column_order()
    w_units = [w_in[:, c].reshape(KT, P, P).transpose(1, 0, 2).reshape(P, KT * P) for c in cols]
    wo = w_out[np.concatenate(mixing_order())].reshape(4, 2, P, 2, 512)
    w_units += [wo[kp, :, :, half].transpose(1, 0, 2).reshape(P, 1024) for half in range(2) for kp in range(4)]
    params = np.concatenate([
        np.asarray(b_in)[0][np.stack(cols)].T,
        np.asarray(lb_logits)[0].reshape(A_HEADS, P).T,
        np.asarray(a_norm_gain)[0].reshape(A_HEADS, P).T,
        np.asarray(pool_scale)[0].reshape(B_TILES, P).T,
        np.repeat(np.repeat(np.asarray(attn_sinks)[0].reshape(KV, 2).T, HD, axis=0), 2, axis=1),
    ], axis=1)
    arrays = {"xt": xt, "xr": xr, "w": np.stack(w_units), "params": params, "consts": constants(),
              "pool_w": np.asarray(pool_w)[0], "b_out": np.asarray(b_out)[0], "ln_gain": np.asarray(ln_gain)[0],
              "ln_bias": np.asarray(ln_bias)[0]}
    arrays = {name: np.ascontiguousarray(a) for name, a in arrays.items()}
    nc = _bacc.Bacc("TRN2", target_bir_lowering=False, num_devices=1)
    args = [nc.dram_tensor(name, a.shape, mybir.dt.from_np(a.dtype), kind="ExternalInput").ap() for name, a in arrays.items()]
    out = nc.dram_tensor("out", (BLOCKS, ROWS, P, D), F32, kind="ExternalOutput").ap()
    trunk_kernel(nc, *args, out)
    r = _run(nc, [arrays], core_ids=[0])
    return r.results[0]["out"].reshape(1, SEQ, D)
```
